# Optimizing a Trainium2 kernel written in Bass

```python
import math, functools
import jax, jax.numpy as jnp
from jax import lax
import numpy as np

D_MODEL = 2048
BATCH = 1
SEQ = 512
DEPTH = 1

CHUNK = 64
QBLK = 128
N_MIXERS = 3
EPS = 1e-6
MLA_HEADS = 16
MLA_Q_LORA = 512
MLA_KV_LORA = 512
MLA_NOPE = 128
MLA_ROPE = 64
MLA_V = 128
ROPE_THETA = 10000.0
CONV_WIDTH = 3
SSM_D_INNER = 2 * D_MODEL
SSM_HEAD_DIM = 64
SSM_HEADS = SSM_D_INNER // SSM_HEAD_DIM
SSM_GROUPS = 8
SSM_STATE = 128
SSM_CONV = 4
SSM_CONV_DIM = SSM_D_INNER + 2 * SSM_GROUPS * SSM_STATE
SSM_IN_DIM = 2 * SSM_D_INNER + 2 * SSM_GROUPS * SSM_STATE + SSM_HEADS
MLP_HIDDEN = 4 * D_MODEL
N_MLA_LAYERS = len(range(0, DEPTH, N_MIXERS))
N_CONV_LAYERS = len(range(1, DEPTH, N_MIXERS))
N_SSM_LAYERS = len(range(2, DEPTH, N_MIXERS))

kernel_name = "hybrid_mla_shortconv_ssd_trunk"

def rms(x):
    xf = x.astype(jnp.float32)
    return (xf * lax.rsqrt(jnp.mean(xf * xf, axis=-1, keepdims=True) + EPS)).astype(x.dtype)

def rmsnorm(x, g):
    return rms(x) * g

def causal_dwconv(u, w):
    k, ch = w.shape
    return lax.conv_general_dilated(
        u, w[:, None, :], window_strides=(1,), padding=[(k - 1, 0)],
        dimension_numbers=("NWC", "WIO", "NWC"), feature_group_count=ch)

def rope_tables(positions):
    inv_freq = ROPE_THETA ** (-jnp.arange(0, MLA_ROPE, 2, dtype=jnp.float32) / MLA_ROPE)
    ang = positions.astype(jnp.float32)[..., None] * inv_freq
    return jnp.cos(ang)[:, :, None, :], jnp.sin(ang)[:, :, None, :]

def apply_rope(t, cos, sin):
    t1, t2 = jnp.split(t, 2, axis=-1)
    return jnp.concatenate([t1 * cos - t2 * sin, t2 * cos + t1 * sin], axis=-1).astype(t.dtype)

def chunk_causal_attention(q, k, v):
    b, s, h, dqk = q.shape
    nblk = s // QBLK
    scale = 1.0 / math.sqrt(dqk)
    key_chunk = jnp.arange(s) // CHUNK
    q_blocks = q.reshape(b, nblk, QBLK, h, dqk).transpose(1, 0, 2, 3, 4)

    def attend(args):
        qb, bi = args
        q_chunk = (bi * QBLK + jnp.arange(QBLK)) // CHUNK
        mask = key_chunk[None, :] <= q_chunk[:, None]
        sc = jnp.einsum("bqhd,bkhd->bhqk", qb, k).astype(jnp.float32) * scale
        sc = jnp.where(mask[None, None], sc, -jnp.inf)
        p = jax.nn.softmax(sc, axis=-1).astype(v.dtype)
        return jnp.einsum("bhqk,bkhd->bqhd", p, v)

    out = lax.map(attend, (q_blocks, jnp.arange(nblk)))
    return out.transpose(1, 0, 2, 3, 4).reshape(b, s, h * v.shape[-1])

def mla_mixer(h, cos, sin, w_down, q_norm, w_uq, kv_norm, w_ukv, w_o):
    b, s, _ = h.shape
    down = h @ w_down
    cq = down[..., :MLA_Q_LORA]
    ckv = down[..., MLA_Q_LORA:MLA_Q_LORA + MLA_KV_LORA]
    k_rope = down[..., MLA_Q_LORA + MLA_KV_LORA:]
    q = (rmsnorm(cq, q_norm) @ w_uq).reshape(b, s, MLA_HEADS, MLA_NOPE + MLA_ROPE)
    kv = (rmsnorm(ckv, kv_norm) @ w_ukv).reshape(b, s, MLA_HEADS, MLA_NOPE + MLA_V)
    q = jnp.concatenate([q[..., :MLA_NOPE], apply_rope(q[..., MLA_NOPE:], cos, sin)], axis=-1)
    k_rope = apply_rope(k_rope[:, :, None, :], cos, sin)
    k = jnp.concatenate([kv[..., :MLA_NOPE],
                         jnp.broadcast_to(k_rope, (b, s, MLA_HEADS, MLA_ROPE))], axis=-1)
    v = kv[..., MLA_NOPE:]
    return chunk_causal_attention(q, k, v) @ w_o

def shortconv_mixer(h, w_in, conv_w, w_out):
    gb, gc, u = jnp.split(h @ w_in, 3, axis=-1)
    return (gb * causal_dwconv(gc * u, conv_w)) @ w_out

def ssd_scan(x, dt, a, bm, cm):
    b, s, nh, p = x.shape
    nc, L, G, hg = s // CHUNK, CHUNK, SSM_GROUPS, nh // SSM_GROUPS
    xf = x.astype(jnp.float32).reshape(b, nc, L, G, hg, p)
    dtc = dt.reshape(b, nc, L, G, hg)
    a_cum = jnp.cumsum(dtc * a.reshape(G, hg), axis=2)
    xdt = xf * dtc[..., None]
    bf = bm.astype(jnp.float32).reshape(b, nc, L, G, SSM_STATE)
    cf = cm.astype(jnp.float32).reshape(b, nc, L, G, SSM_STATE)
    idx = jnp.arange(L)
    causal = idx[:, None] >= idx[None, :]
    seg = a_cum[:, :, :, None] - a_cum[:, :, None, :]
    decay = jnp.exp(jnp.where(causal[:, :, None, None], seg, -jnp.inf))
    cb = jnp.einsum("bclgn,bcsgn->bclsg", cf, bf)
    y_diag = jnp.einsum("bclsg,bclsgh,bcsghp->bclghp", cb, decay, xdt)
    decay_to_end = jnp.exp(a_cum[:, :, -1:] - a_cum)
    states = jnp.einsum("bclgn,bclgh,bclghp->bcghpn", bf, decay_to_end, xdt)
    chunk_decay = jnp.exp(a_cum[:, :, -1])

    def step(carry, inp):
        dec, st = inp
        return carry * dec[..., None, None] + st, carry

    init = jnp.zeros((b, G, hg, p, SSM_STATE), jnp.float32)
    _, prev = lax.scan(step, init, (jnp.moveaxis(chunk_decay, 1, 0), jnp.moveaxis(states, 1, 0)))
    prev = jnp.moveaxis(prev, 0, 1)
    y_off = jnp.einsum("bclgn,bcghpn,bclgh->bclghp", cf, prev, jnp.exp(a_cum))
    return (y_diag + y_off).reshape(b, s, nh, p).astype(x.dtype)

def ssd_mixer(h, w_in, conv_w, conv_b, dt_bias, a_log, d_skip, norm_w, w_out):
    b, s, _ = h.shape
    zxbcdt = h @ w_in
    z = zxbcdt[..., :SSM_D_INNER]
    xbc = zxbcdt[..., SSM_D_INNER:SSM_D_INNER + SSM_CONV_DIM]
    dt = zxbcdt[..., SSM_D_INNER + SSM_CONV_DIM:]
    xbc = jax.nn.silu(causal_dwconv(xbc, conv_w) + conv_b)
    gn = SSM_GROUPS * SSM_STATE
    xs = xbc[..., :SSM_D_INNER].reshape(b, s, SSM_HEADS, SSM_HEAD_DIM)
    bm = xbc[..., SSM_D_INNER:SSM_D_INNER + gn].reshape(b, s, SSM_GROUPS, SSM_STATE)
    cm = xbc[..., SSM_D_INNER + gn:].reshape(b, s, SSM_GROUPS, SSM_STATE)
    dt = jax.nn.softplus(dt.astype(jnp.float32) + dt_bias.astype(jnp.float32))
    a = -jnp.exp(a_log.astype(jnp.float32))
    y = ssd_scan(xs, dt, a, bm, cm) + xs * d_skip[:, None]
    y = y.reshape(b, s, SSM_D_INNER) * jax.nn.silu(z)
    y = rms(y.reshape(b, s, SSM_GROUPS, SSM_D_INNER // SSM_GROUPS)).reshape(b, s, SSM_D_INNER) * norm_w
    return y @ w_out

def squared_relu_mlp(h, w_up, w_down):
    return jnp.square(jax.nn.relu(h @ w_up)) @ w_down

def sublayer(x, c_act, w_ada, b_ada, g_pre, g_post, fn):
    shift, scale, gate = jnp.split(c_act @ w_ada + b_ada, 3, axis=-1)
    h = rmsnorm(x, g_pre) * (1 + scale[:, None, :]) + shift[:, None, :]
    return x + gate[:, None, :] * rmsnorm(fn(h), g_post)

def setup_inputs(seed: int = 0) -> dict:
    key = jax.random.key(seed)
    ks = jax.random.split(key, 32)
    D = D_MODEL
    f32 = jnp.float32

    def nrm(k, shape, fan_in):
        return jax.random.normal(k, shape, f32) * fan_in ** -0.5

    def gain(k, shape):
        return 1.0 + 0.05 * jax.random.normal(k, shape, f32)

    x = jax.random.normal(ks[0], (BATCH, SEQ, D), f32)
    c = jax.random.normal(ks[1], (BATCH, D), f32)
    positions = (jax.random.randint(ks[2], (BATCH, 1), 0, 1024, jnp.int32)
                 + jnp.arange(SEQ, dtype=jnp.int32)[None, :])
    ada_w = nrm(ks[3], (DEPTH, 2, D, 3 * D), D)
    ada_b = 0.02 * jax.random.normal(ks[4], (DEPTH, 2, 3 * D), f32)
    norm_pre = gain(ks[5], (DEPTH, 2, D))
    norm_post = gain(ks[6], (DEPTH, 2, D))
    NA, NB, NC = N_MLA_LAYERS, N_CONV_LAYERS, N_SSM_LAYERS
    mla_w_down = nrm(ks[7], (NA, D, MLA_Q_LORA + MLA_KV_LORA + MLA_ROPE), D)
    mla_q_norm = gain(ks[8], (NA, MLA_Q_LORA))
    mla_w_uq = nrm(ks[9], (NA, MLA_Q_LORA, MLA_HEADS * (MLA_NOPE + MLA_ROPE)), MLA_Q_LORA)
    mla_kv_norm = gain(ks[10], (NA, MLA_KV_LORA))
    mla_w_ukv = nrm(ks[11], (NA, MLA_KV_LORA, MLA_HEADS * (MLA_NOPE + MLA_V)), MLA_KV_LORA)
    mla_w_o = nrm(ks[12], (NA, MLA_HEADS * MLA_V, D), MLA_HEADS * MLA_V)
    conv_w_in = nrm(ks[13], (NB, D, 3 * D), D)
    conv_w = nrm(ks[14], (NB, CONV_WIDTH, D), CONV_WIDTH)
    conv_w_out = nrm(ks[15], (NB, D, D), D)
    ssm_w_in = nrm(ks[16], (NC, D, SSM_IN_DIM), D)
    ssm_conv_w = nrm(ks[17], (NC, SSM_CONV, SSM_CONV_DIM), SSM_CONV)
    ssm_conv_b = 0.02 * jax.random.normal(ks[18], (NC, SSM_CONV_DIM), f32)
    dt0 = jnp.exp(jax.random.uniform(ks[19], (NC, SSM_HEADS), f32,
                                     minval=math.log(1e-3), maxval=math.log(1e-1)))
    ssm_dt_bias = dt0 + jnp.log(-jnp.expm1(-dt0))
    ssm_a_log = jnp.log(jax.random.uniform(ks[20], (NC, SSM_HEADS), f32, minval=1.0, maxval=16.0))
    ssm_d = 1.0 + 0.1 * jax.random.normal(ks[21], (NC, SSM_HEADS), f32)
    ssm_norm = gain(ks[22], (NC, SSM_D_INNER))
    ssm_w_out = nrm(ks[23], (NC, SSM_D_INNER, D), SSM_D_INNER)
    mlp_up = nrm(ks[24], (DEPTH, D, MLP_HIDDEN), D)
    mlp_down = nrm(ks[25], (DEPTH, MLP_HIDDEN, D), MLP_HIDDEN)
    return {"x": x, "c": c, "positions": positions, "ada_w": ada_w, "ada_b": ada_b,
            "norm_pre": norm_pre, "norm_post": norm_post,
            "mla_w_down": mla_w_down, "mla_q_norm": mla_q_norm, "mla_w_uq": mla_w_uq,
            "mla_kv_norm": mla_kv_norm, "mla_w_ukv": mla_w_ukv, "mla_w_o": mla_w_o,
            "conv_w_in": conv_w_in, "conv_w": conv_w, "conv_w_out": conv_w_out,
            "ssm_w_in": ssm_w_in, "ssm_conv_w": ssm_conv_w, "ssm_conv_b": ssm_conv_b,
            "ssm_dt_bias": ssm_dt_bias, "ssm_a_log": ssm_a_log, "ssm_d": ssm_d,
            "ssm_norm": ssm_norm, "ssm_w_out": ssm_w_out,
            "mlp_up": mlp_up, "mlp_down": mlp_down}

def reference(x, c, positions, ada_w, ada_b, norm_pre, norm_post,
              mla_w_down, mla_q_norm, mla_w_uq, mla_kv_norm, mla_w_ukv, mla_w_o,
              conv_w_in, conv_w, conv_w_out,
              ssm_w_in, ssm_conv_w, ssm_conv_b, ssm_dt_bias, ssm_a_log, ssm_d, ssm_norm, ssm_w_out,
              mlp_up, mlp_down):
    c_act = jax.nn.silu(c)
    cos, sin = rope_tables(positions)
    for i in range(DEPTH):
        kind, j = i % N_MIXERS, i // N_MIXERS
        if kind == 0:
            mixer = functools.partial(mla_mixer, cos=cos, sin=sin, w_down=mla_w_down[j],
                                      q_norm=mla_q_norm[j], w_uq=mla_w_uq[j], kv_norm=mla_kv_norm[j],
                                      w_ukv=mla_w_ukv[j], w_o=mla_w_o[j])
        elif kind == 1:
            mixer = functools.partial(shortconv_mixer, w_in=conv_w_in[j], conv_w=conv_w[j],
                                      w_out=conv_w_out[j])
        else:
            mixer = functools.partial(ssd_mixer, w_in=ssm_w_in[j], conv_w=ssm_conv_w[j],
                                      conv_b=ssm_conv_b[j], dt_bias=ssm_dt_bias[j], a_log=ssm_a_log[j],
                                      d_skip=ssm_d[j], norm_w=ssm_norm[j], w_out=ssm_w_out[j])
        x = sublayer(x, c_act, ada_w[i, 0], ada_b[i, 0], norm_pre[i, 0], norm_post[i, 0], mixer)
        mlp = functools.partial(squared_relu_mlp, w_up=mlp_up[i], w_down=mlp_down[i])
        x = sublayer(x, c_act, ada_w[i, 1], ada_b[i, 1], norm_pre[i, 1], norm_post[i, 1], mlp)
    return x


_drawn_inputs = setup_inputs


def setup_inputs(seed=0):
    import zlib

    import numpy as np

    out = dict(_drawn_inputs(seed))
    spreads = {}
    factors = {'mla_q_norm': 8.0}
    for name, (base, spread) in spreads.items():
        noise = np.random.default_rng([zlib.crc32(name.encode()), seed]).standard_normal(out[name].shape)
        drawn = base * np.exp(spread * noise) if base else spread * noise
        out[name] = __import__('jax').numpy.asarray(drawn.astype(out[name].dtype))
    for name, factor in factors.items():
        out[name] = (out[name] * factor).astype(out[name].dtype)
    return out
```

```python
from contextlib import ExitStack

import concourse.bass as bass
from concourse import mybir

F32 = mybir.dt.float32
F32R = mybir.dt.float32r
I32 = mybir.dt.int32
ALU = mybir.AluOpType
ACT = mybir.ActivationFunctionType
AX_X = mybir.AxisListType.X

P = 128
D = 2048
KT = D // P
TOK = 512
TT = TOK // P
LORA = 512
LT = LORA // P
HEADS = 16
NOPE = 128
ROPE = 64
HALF = ROPE // 2
VDIM = 128
QD = NOPE + ROPE
KVD = NOPE + VDIM
PAIRS = HEADS // 2
HIDDEN = 4 * D
CH = 512
CHUNKS = HIDDEN // CH
SCALE = float(QD) ** -0.5
EPS = 1e-6
MASKED = -1.0e30
ADA = 3 * D
Q_PARTS = 6
UNIT = 2048

U_A = [0, 2, 4, 6]
U_B = [1, 3, 5, 7]
U_C = [8, 9]
U_ATT = 10
U_MLP = 12 + 4 * (PAIRS - 1) + 2


def u_pair(p):
    return U_ATT if isinstance(p, int) and p == 0 else 8 + 4 * p


N_B = 2 * ADA // P
C_B = 0
C_C = N_B
C_PRE = C_C + KT
C_POST = C_PRE + 2 * KT
C_QN = C_POST + 2 * KT
C_KVN = C_QN + LT
N_PC = C_KVN + LT

S_QN, S_KN, S_QR, S_V, S_PT, S_AO = (0, 2), (4, 6), (8, 9), (10, 12), (14, 18), (22, 24)

S_AT = [(3, 384), (4, 0), (3, 0), (2, 0)]
P_AT = [0, 128, 384, 768]
ROPE_A, ROPE_B = 1280, 1792
T_ORDER = [2, 0, 1, 3]


def t_at(i, head):
    return [(6, 384), ((7, 4)[head], 0), (6, 0), (5, 0)][i]


def trunk(nc, x, c, positions, ada_w, ada_b, norm_pre, norm_post, w_down, q_norm, w_uq, kv_norm,
          w_ukv, w_o, mlp_up, mlp_down, inv_freq, out):
    ctx = ExitStack()

    def sb(name, shape, dt=F32):
        return ctx.enter_context(nc.sbuf_tensor(name, shape, dt))

    def sem(name):
        return ctx.enter_context(nc.semaphore(name))

    big = sb("big", [P, 32, 512], F32R)
    y = sb("y", [P, TT, D])
    lat = sb("lat", [P, 2, 8, 512], F32R)
    raw = sb("raw", [P, 2, UNIT])
    split = sb("split", [P, 2, 2, UNIT], F32R)
    ada = sb("ada", [P, 2, UNIT])
    scr = sb("scr", [P, 5 * 512])
    krope = sb("krope", [P, 2, 2, 512], F32R)
    trig = sb("trig", [P, 2, TOK])
    acc = sb("acc", [P, 2, 512])
    ident = sb("ident", [P, P])
    ones = sb("ones", [P, P])
    mask_u = sb("mask_u", [P, P], F32R)
    mask_v = sb("mask_v", [P, P], F32R)
    pcol = sb("pcol", [P, N_PC])
    csil = sb("csil", [P, 2, KT])
    mod = sb("mod", [P, 2, 2, KT])
    sums = sb("sums", [P, 2, 2 * KT])
    gate = sb("gate", [P, 2, KT])
    stat = sb("stat", [P, 32])
    ps = ctx.enter_context(nc.psum_tensor("ps", [P, 8, 512], F32))

    x1_dram = nc.dram_tensor("x1_scratch", [TOK, D], F32, kind="Internal").ap()
    gate_dram = nc.dram_tensor("gate_scratch", [2, D], F32, kind="Internal").ap()

    par_full = sem("par_full")
    x_full = [sem(f"x_full{t}") for t in range(TT)]
    q_full = sem("q_full")
    raw_full = [sem(f"raw_full{s}") for s in range(2)]
    ada_full = [sem(f"ada_full{s}") for s in range(2)]
    consts = sem("consts")
    ones_done = sem("ones_done")
    hi_done, lo_done, unit_used = sem("hi_done"), sem("lo_done"), sem("unit_used")
    ada_step = sem("ada_step")
    col_ps, col_saved = sem("col_ps"), sem("col_saved")
    par_ps, par_cols = sem("par_ps"), sem("par_cols")
    dve_own = sem("dve_own")
    c_exp = sem("c_exp")
    ss_done, var_done, sd_done, xn_done = sem("ss_done"), sem("var_done"), sem("sd_done"), sem("xn_done")
    xt_ps, xt_out = sem("xt_ps"), sem("xt_out")
    mod_done, h_hi, h_lo = sem("mod_done"), sem("h_hi"), sem("h_lo")
    down_ps, sq_done, lat_sum = sem("down_ps"), sem("sq_done"), sem("lat_sum")
    lat_var, lat_sd, lat_mul, lat_hi, lat_lo = (sem(n) for n in ("lat_var", "lat_sd", "lat_mul", "lat_hi", "lat_lo"))
    ang_done, trig_done = sem("ang_done"), sem("trig_done")
    kr_ps, kr_rot, kr_hi, kr_lo = sem("kr_ps"), sem("kr_rot"), sem("kr_hi"), sem("kr_lo")
    y_zero = sem("y_zero")
    pj_ps, pj_hi, pj_lo, q_rot = sem("pj_ps"), sem("pj_hi"), sem("pj_lo"), sem("q_rot")
    s_ps, s_max, nbias, s_exp, p_norm = (sem(n) for n in ("s_ps", "s_max", "nbias", "s_exp", "p_norm"))
    t_ps, t_hi, t_lo, pv_ps, ao_hi, ao_lo = (sem(n) for n in ("t_ps", "t_hi", "t_lo", "pv_ps", "ao_hi", "ao_lo"))
    wo_ps, wo_added = sem("wo_ps"), sem("wo_added")
    gate_done, gate_put, gate_full = sem("gate_done"), sem("gate_put"), sem("gate_full")
    res_full = [sem(f"res_full{s}") for s in range(2)]
    res_added, x1_put = sem("res_added"), sem("x1_put")
    up_ps, act_relu, act_sq, hid_hi, hid_lo = (sem(n) for n in ("up_ps", "act_relu", "act_sq", "hid_hi", "hid_lo"))
    dn_ps, dn_added = sem("dn_ps"), sem("dn_added")
    out_put = sem("out_put")

    x2 = x.rearrange("b s d -> (b s) d")
    out2 = out.rearrange("b s d -> (b s) d")
    w_dn, w_q, w_kv, w_out = w_down[0], w_uq[0], w_ukv[0], w_o[0]
    up, dn = mlp_up[0], mlp_down[0]
    xt_view = y[:].rearrange("p t (k c) -> p k t c", c=P)

    def rows(w, r0, n, c0, cols):
        return w[r0:r0 + n * P, c0:c0 + cols].rearrange("(k p) n -> p k n", p=P)

    def raw_of(u, n, cols):
        return raw[:, u % 2, :n * cols].rearrange("p (k n) -> p k n", k=n)

    def halves(s, n, cols):
        return [split[:, s, i, :n * cols].rearrange("p (k n) -> p k n", k=n) for i in (0, 1)]

    def product(o, st, mv, first, last):
        nc.tensor.matmul(o, st[0], mv[1], start=first, stop=False)
        nc.tensor.matmul(o, st[0], mv[0], start=False, stop=False)
        return nc.tensor.matmul(o, st[1], mv[0], start=False, stop=last)

    def h_of(k):
        return big[:, k, :], big[:, 16 + k, :]

    def res_tile(t):
        return ada[:, 1, :] if t % 2 == 0 else scr[:, 0:D]

    def c_parts(slot):
        r = raw[:, slot, :8 * 192].rearrange("p (k n) -> p k n", k=8)
        s = [split[:, slot, i, :].rearrange("p (k n) -> p k n", k=8) for i in (0, 1)]
        parts = [(r[:, :, 0:P], [s[0][:, :, 0:P], s[1][:, :, 0:P]])]
        r2 = r[:, :, P:192].rearrange("p k (h e) -> p k h e", h=2)
        s2 = [v[:, :, P:256].rearrange("p k (h d e) -> p k h d e", h=2, d=2) for v in s]
        for d in (0, 1):
            parts.append((r2, [v[:, :, :, d, :] for v in s2]))
        return parts

    def raw_count(u, slot):
        n = 8 * (u - slot) + 16
        if slot == 0 and not (isinstance(u, int) and u < U_ATT):
            n -= 16 * (PAIRS + 1)
        return n

    def v_view(i):
        return big[:, S_V[i]:S_V[i] + 2, :].rearrange("p s (t n) -> p (s t) n", t=2)

    block = ctx.enter_context(nc.Block())

    @block.sync
    def _(sp):
        def unit(u, src_list, slot, full=None):
            if not isinstance(u, int) or u >= 2:
                sp.wait_ge(lo_done, u - 1)
            for dst, src in src_list:
                sp.dma_start(dst, src).then_inc(full or raw_full[slot], 16)

        def ada_unit(m, slot, src):
            if not isinstance(m, int) or m >= 2:
                sp.wait_ge(ada_step, 4 * (m - 1))
            sp.dma_start(ada[:, slot, :].rearrange("p (k n) -> p k n", k=4), src).then_inc(ada_full[slot], 16)

        b_rows = ada_b.rearrange("l s (r e) -> (l s r) e", e=P)
        sp.dma_start(scr[0:KT, P:2 * P], c.rearrange("b (r e) -> (b r) e", e=P)).then_inc(par_full, 16)
        sp.dma_start(scr[0:N_B, 0:P], b_rows).then_inc(par_full, 16)
        o = KT
        for a, n in ((norm_pre.rearrange("l s (r e) -> (l s r) e", e=P), 2 * KT),
                     (norm_post.rearrange("l s (r e) -> (l s r) e", e=P), 2 * KT),
                     (q_norm.rearrange("l (r e) -> (l r) e", e=P), LT),
                     (kv_norm.rearrange("l (r e) -> (l r) e", e=P), LT)):
            sp.dma_start(scr[o:o + n, P:2 * P], a).then_inc(par_full, 16)
            o += n
        sp.dma_start(stat[:, 0:1], inv_freq).then_inc(par_full, 16)
        sp.dma_start(scr[:, 512:1024].bitcast(I32), positions.broadcast_to([P, TOK])).then_inc(par_full, 16)
        for t in range(TT):
            sp.dma_start(y[:, t, :], x2[t * P:(t + 1) * P, :]).then_inc(x_full[t], 16)

        m = 0
        for kk in range(4):
            for part in (0, 1):
                for r in range(4):
                    ada_unit(m, m % 2, rows(ada_w[0, 0], r * 512, 4, part * D + kk * 512, 512))
                    m += 1
            unit(U_A[kk], [(raw_of(0, 4, 512), rows(w_dn, kk * 512, 4, 0, 512))], 0)
            unit(U_B[kk], [(raw_of(1, 4, 384), rows(w_dn, kk * 512, 4, 512, 384))], 1)
        for i in (0, 1):
            unit(U_C[i], [(raw_of(i, 8, 192), rows(w_dn, i * 1024, 8, 896, 192))], i)

        def ada_two(p, a):
            for i in (0, 1):
                if a < 4:
                    src = ada_w[0, 1][(a + i) * 512:(a + i + 1) * 512, bass.ds(p * 512, 512)]
                else:
                    layer, col = p // (PAIRS // 2), 2 * D + (p % (PAIRS // 2)) * 512
                    src = ada_w[0][bass.ds(layer, 1), (a + i - 4) * 512:(a + i - 3) * 512, bass.ds(col, 512)]
                    src = src.rearrange("s r n -> (s r) n")
                ada_unit(32 + 8 * p + a + i, i, src.rearrange("(k p) n -> p k n", p=P))

        def pair_units(p, before=None):
            u = u_pair(p)
            first = isinstance(p, int) and p == 0
            q_src = w_q[:, bass.ds(p * (2 * QD), 2 * QD)].rearrange("(k p) n -> p k n", p=P)
            kv_col = 0 if first else (before * 2 + 2) * KVD
            kv_src = w_kv[:, bass.ds(kv_col, 2 * KVD)].rearrange("(k p) n -> p k n", p=P)
            q_dst = raw_of(0, 4, 2 * QD)
            parts = []
            for d in (0, 1):
                parts.append((q_dst[:, :, P * (1 + d):P * (2 + d)], q_src[:, :, QD * d:QD * d + NOPE]))
                for h in (0, 1):
                    o, i = HALF * (2 * h + d), QD * d + NOPE + HALF * h
                    parts.append((q_dst[:, :, o:o + HALF], q_src[:, :, i:i + HALF]))
            with nc.allow_non_contiguous_dma(reason="the rotary columns are runs of 128 bytes"):
                unit(u, parts, 0, q_full)
            if not first:
                ada_two(before, 6)
            unit(u + 1, [(raw_of(1, 4, 2 * KVD), kv_src)], 1)
            ada_two(p, 0)
            if not first:
                o_rows = w_out[bass.ds(before * 256, 256), :].rearrange("(k p) n -> p k n", p=P)
                unit(u + 2, [(raw_of(0, 2, 1024), o_rows[:, :, 0:1024])], 0)
            ada_two(p, 2)
            if not first:
                unit(u + 3, [(raw_of(1, 2, 1024), o_rows[:, :, 1024:2048])], 1)
            ada_two(p, 4)

        pair_units(0)
        with sp.Fori(0, PAIRS - 1) as before:
            pair_units(before + 1, before)
        last = rows(w_out, (PAIRS - 1) * 256, 2, 0, D)
        cuts = [(k, a, b) for k in (0, 1) for a, b in ((0, 512), (512, 768), (768, 1024))]
        unit(U_MLP - 2, [(raw_of(0, 2, 1024)[:, k, a:b], last[:, k, a:b]) for k, a, b in cuts], 0, q_full)
        ada_two(PAIRS - 1, 6)
        unit(U_MLP - 1, [(raw_of(1, 2, 1024), last[:, :, 1024:])], 1)

        def gate_rows(s):
            sp.wait_ge(gate_done, s + 1)
            with nc.allow_non_contiguous_dma(reason="one word per partition and tile, 8 KB in all"):
                sp.dma_start(gate_dram[s].rearrange("(k p) -> p k", p=P), gate[:, s, :]).then_inc(gate_put, 16)
            sp.wait_ge(gate_put, 16 * (s + 1))
            sp.dma_start(ada[:, 0, :], gate_dram[s:s + 1, :].broadcast_to([P, D])).then_inc(gate_full, 16)

        def up_unit(c, kk):
            src = up[kk * 512:(kk + 1) * 512, bass.ds(c * CH, CH)]
            unit(U_MLP + 8 * c + kk, [(raw_of(kk, 4, 512), src.rearrange("(k p) n -> p k n", p=P))], kk % 2)

        def down_unit(c, n):
            src = dn[bass.ds(c * CH, CH), n * 512:(n + 1) * 512]
            unit(U_MLP + 8 * c + 4 + n, [(raw_of(n, 4, 512), src.rearrange("(k p) n -> p k n", p=P))], n % 2)

        gate_rows(0)
        up_unit(0, 0)
        up_unit(0, 1)
        sp.wait_ge(t_ps, 2 * PAIRS)
        for t in range(TT):
            if t >= 2:
                sp.wait_ge(xt_ps, KT + 4 * (t - 1))
            sp.dma_start(res_tile(t), x2[t * P:(t + 1) * P, :]).then_inc(res_full[t % 2], 16)
            if t >= 1:
                sp.wait_ge(res_added, t)
                sp.dma_start(x1_dram[(t - 1) * P:t * P, :], y[:, t - 1, :]).then_inc(x1_put, 16)
        sp.wait_ge(res_added, TT)
        sp.dma_start(x1_dram[(TT - 1) * P:, :], y[:, TT - 1, :]).then_inc(x1_put, 16)

        for kk in (2, 3):
            up_unit(0, kk)
        for n in range(4):
            down_unit(0, n)
        with sp.Fori(1, CHUNKS) as c_:
            for kk in range(4):
                up_unit(c_, kk)
            for n in range(4):
                down_unit(c_, n)
        sp.wait_ge(xt_ps, KT + 4 * TT)
        gate_rows(1)
        sp.wait_ge(x1_put, 16 * TT)
        sp.wait_ge(hid_lo, 4 * CHUNKS)
        for t in range(TT):
            if t >= 2:
                sp.wait_ge(res_added, TT + t - 1)
            sp.dma_start(res_tile(t), x1_dram[t * P:(t + 1) * P, :]).then_inc(res_full[t % 2], 16)
            if t >= 1:
                sp.wait_ge(res_added, TT + t)
                sp.dma_start(out2[(t - 1) * P:t * P, :], y[:, t - 1, :]).then_inc(out_put, 16)
        sp.wait_ge(res_added, 2 * TT)
        sp.dma_start(out2[(TT - 1) * P:, :], y[:, TT - 1, :]).then_inc(out_put, 16)
        sp.wait_ge(out_put, 16 * TT)


    @block.gpsimd
    def _(pool):
        nc.gpsimd.memset(ident[:], 0.0).then_inc(consts, 1)
        nc.gpsimd.memset(mask_u[:].bitcast(F32), 0.0).then_inc(consts, 1)
        nc.gpsimd.memset(mask_v[:].bitcast(F32), 0.0).then_inc(consts, 1)
        nc.gpsimd.memset(krope[:].bitcast(F32), 0.0).then_inc(consts, 1)
        pool.wait_ge(consts, 4)
        nc.gpsimd.affine_select(out=ident[:], in_=ident[:], compare_op=ALU.not_equal, fill=1.0, base=0,
                                pattern=[[-1, P]], channel_multiplier=1).then_inc(consts, 1)
        nc.gpsimd.memset(mask_u[0:1, 0:64].bitcast(F32), 1.0).then_inc(consts, 1)
        nc.gpsimd.memset(mask_v[0:1, 64:128].bitcast(F32), MASKED).then_inc(consts, 1)

        def lo(u, slot, words=UNIT):
            pool.wait_ge(hi_done, u + 1)
            nc.gpsimd.tensor_tensor(split[:, slot, 1, :words], raw[:, slot, :words],
                                    split[:, slot, 0, :words].bitcast(F32), ALU.subtract).then_inc(lo_done, 1)

        def lo_parts(u, parts):
            pool.wait_ge(hi_done, u + 1)
            for r, s in parts:
                op = nc.gpsimd.tensor_tensor(s[1], r, s[0].bitcast(F32), ALU.subtract)
            op.then_inc(lo_done, 1)

        for u in range(8):
            lo(u, u % 2, 2048 if u % 2 == 0 else 4 * 384)
        for u in (8, 9):
            lo_parts(u, c_parts(u % 2))
        lo(10, 0)
        lo(11, 1)
        with pool.Fori(1, PAIRS) as p:
            for j in range(4):
                lo(u_pair(p) + j, j % 2)
        for j in (0, 1):
            lo(U_MLP - 2 + j, j)
        with pool.Fori(0, CHUNKS) as c_:
            for j in range(8):
                lo(U_MLP + 8 * c_ + j, j % 2)


    @block.scalar
    def _(act):
        def unit_hi(u, slot, used=None, count=None, parts=None, full=None, words=UNIT):
            act.wait_ge(*(full or (raw_full[slot], raw_count(u, slot))))
            if used is not None:
                act.wait_ge(used, count)
            for r, s in parts or [(raw[:, slot, :words], [split[:, slot, 0, :words]])]:
                op = nc.scalar.activation(s[0], r, ACT.Copy)
            op.then_inc(hi_done, 1)

        act.wait_ge(par_cols, 1)
        nc.scalar.activation(csil[:, 1, :], pcol[:, C_C:C_C + KT], ACT.Exp, scale=-1.0).then_inc(c_exp, 1)
        for i in (0, 1):
            act.wait_ge(ang_done, i + 1)
            nc.scalar.activation(trig[:, i, :], trig[:, i, :], ACT.Sin).then_inc(trig_done, 1)

        def row_stats(t, n, source):
            source(t)
            nc.scalar.activation(ps[:, 0:4, :].rearrange("p b n -> p (b n)"), y[:, t, :], ACT.Square,
                                 accum_out=stat[:, 4:5]).then_inc(ss_done, 1)
            act.wait_ge(var_done, n + 1)
            nc.scalar.activation(stat[:, 6:7], stat[:, 5:6], ACT.Sqrt).then_inc(sd_done, 1)

        for t in range(TT):
            row_stats(t, t, lambda t: act.wait_ge(x_full[t], 16))
        for k in range(KT):
            act.wait_ge(xt_ps, k + 1)
            nc.scalar.activation(xt_view[:, k], ps[:, k % 4, :].rearrange("p (t c) -> p t c", t=TT),
                                 ACT.Copy).then_inc(xt_out, 1)

        for kk in range(4):
            for k in range(4 * kk, 4 * kk + 4):
                act.wait_ge(mod_done, k + 1)
                nc.scalar.activation(big[:, k, :].rearrange("p (t c) -> p t c", t=TT), xt_view[:, k],
                                     ACT.Copy).then_inc(h_hi, 1)
            for u in (U_A[kk], U_B[kk]):
                words = 4 * 512 if u % 2 == 0 else 4 * 384
                if u < 2:
                    unit_hi(u, u % 2, words=words)
                else:
                    unit_hi(u, u % 2, unit_used, u - 1, words=words)

        def squares(tiles, n0):
            for j, b in enumerate(tiles):
                n = n0 + j
                act.wait_ge(down_ps, n + 1)
                if n >= 2:
                    act.wait_ge(lat_sum, n - 1)
                nc.scalar.activation(scr[:, (n % 2) * 512:(n % 2 + 1) * 512], ps[:, b, :],
                                     ACT.Square).then_inc(sq_done, 1)

        def latent_hi(n0):
            act.wait_ge(lat_var, n0 // 4 + 1)
            nc.scalar.activation(scr[:, 1024:1536], scr[:, 1024:1536], ACT.Sqrt).then_inc(lat_sd, 1)
            for j in range(4):
                act.wait_ge(lat_mul, n0 + j + 1)
                nc.scalar.activation(lat[:, 0, n0 + j, :], scr[:, (j % 2) * 512:(j % 2 + 1) * 512],
                                     ACT.Copy).then_inc(lat_hi, 1)

        squares(range(4), 0)
        latent_hi(0)
        for i in (0, 1):
            unit_hi(U_C[i], i, down_ps, (4, 7)[i], c_parts(i))
        act.wait_ge(lat_lo, 4)
        squares((4, 5, 6, 0), 4)
        unit_hi(10, 0, unit_used, 7, full=(q_full, 16 * Q_PARTS))
        act.wait_ge(kr_rot, 1)
        for par in (0, 1):
            for half in (0, 1):
                r0 = 64 * half + 32 * par
                op = nc.scalar.activation(krope[r0:r0 + 32, par, 0, :], scr[r0:r0 + 32, ROPE_A:ROPE_A + 512],
                                          ACT.Copy)
        op.then_inc(kr_hi, 1)
        latent_hi(4)
        unit_hi(11, 1, kr_ps, 1)

        def pair(p):
            first = isinstance(p, int) and p == 0
            u = u_pair(p)

            def proj_hi(k, dst, src):
                act.wait_ge(pj_ps, 7 * p + k + 1)
                nc.scalar.activation(dst, src, ACT.Copy).then_inc(pj_hi, 1)

            act.wait_ge(q_rot, p + 1)
            proj_hi(0, big[:, S_QR[0], :], scr[:, ROPE_A:ROPE_A + 512])
            proj_hi(1, big[:, S_QN[0], :], ps[:, 0, :])
            proj_hi(2, big[:, S_QN[0] + 1, :], ps[:, 1, :])
            proj_hi(3, big[:, S_KN[0], :], ps[:, 0, :])
            if not first:
                unit_hi(u + 2, 0, pj_ps, 7 * p + 3, full=(raw_full[0], 16 * (5 + p)))
            proj_hi(4, big[:, S_KN[0] + 1, :], ps[:, 1, :])

            def exps(hd):
                n = 2 * p + hd
                act.wait_ge(nbias, n + 1)
                if not (first and hd == 0):
                    act.wait_ge(t_ps, n)
                for i in range(TT):
                    b, o = S_AT[i]
                    ln = (i + 1) * P
                    op = nc.scalar.activation(scr[:, P_AT[i]:P_AT[i] + ln], ps[:, b, o:o + ln], ACT.Exp,
                                              bias=stat[:, 12 + i:13 + i], scale=SCALE,
                                              accum_out=stat[:, 16 + i:17 + i])
                op.then_inc(s_exp, 1)

            def turned_hi(hd):
                n = 2 * p + hd
                act.wait_ge(t_ps, n + 1)
                if not (first and hd == 0):
                    act.wait_ge(pv_ps, n)
                for i in T_ORDER:
                    dst = big[:, S_PT[0]:S_PT[0] + i + 1, i * P:(i + 1) * P]
                    b, o = t_at(i, hd)
                    src = ps[:, b, o:o + (i + 1) * P].rearrange("p (j c) -> p j c", c=P)
                    nc.scalar.activation(dst, src, ACT.Copy).then_inc(t_hi, 1)

            exps(0)
            proj_hi(5, v_view(0)[:, 0:2], ps[:, 0, :].rearrange("p (t n) -> p t n", t=2))
            proj_hi(6, v_view(0)[:, 2:4], ps[:, 1, :].rearrange("p (t n) -> p t n", t=2))
            if not first:
                unit_hi(u + 3, 1, pj_ps, 7 * p + 7)
            turned_hi(0)
            exps(1)
            if first:
                unit_hi(12, 0, pj_ps, 3, full=(q_full, 16 * Q_PARTS * 2))
            else:
                unit_hi(u + 4, 0, wo_ps, 16 * (p - 1) + 8, full=(q_full, 16 * Q_PARTS * (p + 2)))
            turned_hi(1)
            act.wait_ge(pv_ps, 2 * p + 2)
            for hd in (0, 1):
                nc.scalar.activation(big[:, S_AO[0] + hd, :], ps[:, (7, 4)[hd], :], ACT.Copy).then_inc(ao_hi, 1)
            if first:
                unit_hi(13, 1, pj_ps, 7)
            else:
                unit_hi(u + 5, 1, wo_ps, 16 * p)

        pair(0)
        with act.Fori(1, PAIRS) as p:
            pair(p)

        for i in (0, 1):
            unit_hi(U_MLP + i, i, wo_ps, 16 * (PAIRS - 1) + 8 * (i + 1))
        for tt in range(TT + 1):
            if tt < TT:
                row_stats(tt, TT + 2 * tt, lambda t: act.wait_ge(wo_added, 16 * PAIRS))
                row_stats(tt, TT + 2 * tt + 1, lambda t: act.wait_ge(res_added, t + 1))
            t = tt - 1
            for g in range(4) if t >= 0 else ():
                n = 4 * t + g
                act.wait_ge(mod_done, KT + n + 1)
                nc.scalar.activation(big[:, 4 * g:4 * g + 4, t * P:(t + 1) * P],
                                     acc[:, n % 2, :].rearrange("p (k c) -> p k c", c=P),
                                     ACT.Copy).then_inc(h_hi, 1)

        def mlp(c_):
            u = U_MLP + 8 * c_
            for j in range(2, 5):
                unit_hi(u + j, j % 2, unit_used, 7 + 3 * c_ + j - 1)
            unit_hi(u + 5, 1, up_ps, 4 * c_ + 4)
            for j in range(4):
                n = 4 * c_ + j
                act.wait_ge(up_ps, n + 1)
                if not (isinstance(c_, int) and j < 2):
                    act.wait_ge(act_sq, n - 1)
                nc.scalar.activation(scr[:, (j % 2) * 512:(j % 2 + 1) * 512], ps[:, j, :],
                                     ACT.Relu).then_inc(act_relu, 1)
                act.wait_ge(act_relu, n + 1)
                nc.scalar.activation(lat[:, 0, j, :], scr[:, (j % 2) * 512:(j % 2 + 1) * 512],
                                     ACT.Square).then_inc(hid_hi, 1)
            unit_hi(u + 6, 0, dn_ps, 16 * c_ + 4)
            unit_hi(u + 7, 1, dn_ps, 16 * c_ + 8)

        mlp(0)
        with act.Fori(1, CHUNKS) as c_:
            for j in (0, 1):
                unit_hi(U_MLP + 8 * c_ + j, j, dn_ps, 16 * (c_ - 1) + 12 + 4 * j)
            mlp(c_)
        for t in range(TT):
            row_stats(t, 3 * TT + t, lambda t: act.wait_ge(dn_added, 16 * CHUNKS))


    @block.vector
    def _(dve):
        own = [0]

        def link(op):
            own[0] += 1
            op.then_inc(dve_own, 1)
            dve.wait_ge(dve_own, own[0])

        V = nc.vector
        V.memset(ones[:], 1.0).then_inc(ones_done, 1)
        dve.wait_ge(par_ps, 1)
        V.tensor_copy(pcol[:], ps[:, 7, 0:N_PC]).then_inc(par_cols, 1)
        dve.wait_ge(c_exp, 1)
        link(V.tensor_scalar(csil[:, 1, :], csil[:, 1, :], 1.0, None, ALU.add))
        link(V.reciprocal(csil[:, 0, :], csil[:, 1, :]))
        link(V.tensor_tensor(csil[:, 0, :], pcol[:, C_C:C_C + KT], csil[:, 0, :], ALU.mult))

        dve.wait_ge(par_full, 16 * 8)
        turn = 6.283185307179586
        c1, c2 = 6.28125, 0.0019350051879882812
        c3 = turn - c1 - c2
        ang, cnt = scr[:, 1024:1536], scr[:, 1536:2048]
        link(V.tensor_copy(ang, scr[:, 512:1024].bitcast(I32)))
        link(V.tensor_scalar(ang, ang, stat[:, 0:1], None, ALU.mult))
        for i, shift in ((0, 0.25), (1, 0.0)):
            magic = 12582912.0
            link(V.tensor_scalar(cnt, ang, 1.0 / turn, shift, ALU.mult, ALU.add))
            link(V.tensor_scalar(cnt, cnt, magic, None, ALU.add))
            link(V.tensor_scalar(cnt, cnt, -magic, None, ALU.add))
            link(V.scalar_tensor_tensor(out=trig[:, i, :], in0=cnt, scalar=-c1, in1=ang, op0=ALU.mult, op1=ALU.add))
            link(V.scalar_tensor_tensor(out=trig[:, i, :], in0=cnt, scalar=-c2, in1=trig[:, i, :],
                                        op0=ALU.mult, op1=ALU.add))
            link(V.scalar_tensor_tensor(out=trig[:, i, :], in0=cnt, scalar=-c3, in1=trig[:, i, :],
                                        op0=ALU.mult, op1=ALU.add))
            link(V.tensor_scalar(trig[:, i, :], trig[:, i, :], shift * turn, 3.1415925, ALU.add, ALU.min))
            V.tensor_scalar(trig[:, i, :], trig[:, i, :], -3.1415925, None, ALU.max).then_inc(ang_done, 1)
        dve.wait_ge(trig_done, 2)
        link(V.tensor_scalar(trig[0:64, 1, :], trig[0:64, 1, :], -1.0, None, ALU.mult))

        def row_rstd(n):
            dve.wait_ge(ss_done, n + 1)
            V.tensor_scalar(stat[:, 5:6], stat[:, 4:5], 1.0 / D, EPS, ALU.mult, ALU.add).then_inc(var_done, 1)
            dve.wait_ge(sd_done, n + 1)
            link(V.reciprocal(stat[:, 7:8], stat[:, 6:7]))

        for t in range(TT):
            row_rstd(t)
            V.tensor_scalar(y[:, t, :], y[:, t, :], stat[:, 7:8], None, ALU.mult).then_inc(xn_done, 1)

        def ada_steps(chunk0, s0, s1):
            for s in range(s0, s1):
                slot, k, row, which = (s // 4) % 2, s % 4, s % 16, s // 16
                cols = ada[:, slot, k * 512:(k + 1) * 512]
                if k == 0:
                    dve.wait_ge(ada_full[slot], 16 * (2 * chunk0 + s // 8 + 1))
                if row == 0:
                    if not (isinstance(chunk0, int) and chunk0 == 0):
                        dve.wait_ge(col_ps, chunk0 + which - 1)
                    op = V.tensor_scalar(acc[:, which, :], cols, csil[:, 0, 0:1], None, ALU.mult)
                else:
                    dve.wait_ge(ada_step, 16 * chunk0 + s)
                    op = V.scalar_tensor_tensor(out=acc[:, which, :], in0=cols, scalar=csil[:, 0, row:row + 1],
                                                in1=acc[:, which, :], op0=ALU.mult, op1=ALU.add)
                op.then_inc(ada_step, 1)

        for kk in range(4):
            cols = slice(4 * kk, 4 * kk + 4)
            ada_steps(2 * kk, 0, 32)
            dve.wait_ge(col_ps, 2 * kk + 2)
            V.tensor_tensor(mod[:, 0, 0, cols], ps[:, 7, 0:4], pcol[:, C_B + 4 * kk:C_B + 4 * kk + 4], ALU.add)
            link(V.tensor_tensor(mod[:, 0, 1, cols], ps[:, 7, 4:8],
                                 pcol[:, C_B + KT + 4 * kk:C_B + KT + 4 * kk + 4], ALU.add))
            V.scalar_tensor_tensor(out=mod[:, 0, 1, cols], in0=mod[:, 0, 1, cols], scalar=1.0,
                                   in1=pcol[:, C_PRE + 4 * kk:C_PRE + 4 * kk + 4], op0=ALU.add,
                                   op1=ALU.mult).then_inc(col_saved, 2)
            dve.wait_ge(col_saved, 2 * kk + 2)
            for k in range(4 * kk, 4 * kk + 4):
                dve.wait_ge(xt_out, k + 1)
                V.tensor_scalar(xt_view[:, k], xt_view[:, k], mod[:, 0, 1, k:k + 1], mod[:, 0, 0, k:k + 1],
                                ALU.mult, ALU.add).then_inc(mod_done, 1)
            for k in range(4 * kk, 4 * kk + 4):
                dve.wait_ge(h_hi, k + 1)
                V.tensor_tensor(big[:, 16 + k, :].rearrange("p (t c) -> p t c", t=TT), xt_view[:, k],
                                big[:, k, :].bitcast(F32).rearrange("p (t c) -> p t c", t=TT),
                                ALU.subtract).then_inc(h_lo, 1)

        def latent(n0, tiles, gcol):
            rs = scr[:, 1024:1536]
            dve.wait_ge(lat_sum, n0 + 4)
            V.tensor_scalar(rs, ps[:, 7, :], 1.0 / LORA, EPS, ALU.mult, ALU.add).then_inc(lat_var, 1)
            dve.wait_ge(lat_sd, n0 // 4 + 1)
            link(V.reciprocal(scr[:, 1536:2048], rs))
            for j, b in enumerate(tiles):
                tmp = scr[:, (j % 2) * 512:(j % 2 + 1) * 512]
                V.scalar_tensor_tensor(out=tmp, in0=ps[:, b, :], scalar=pcol[:, gcol + j:gcol + j + 1],
                                       in1=scr[:, 1536:2048], op0=ALU.mult, op1=ALU.mult).then_inc(lat_mul, 1)
                dve.wait_ge(lat_hi, n0 + j + 1)
                V.tensor_tensor(lat[:, 1, n0 + j, :], tmp, lat[:, 0, n0 + j, :].bitcast(F32),
                                ALU.subtract).then_inc(lat_lo, 1)

        def rotate(b, done):
            A, B = scr[:, ROPE_A:ROPE_A + 512], scr[:, ROPE_B:ROPE_B + 512]
            V.tensor_tensor(A, ps[:, b, :], trig[:, 0, :], ALU.mult)
            V.tensor_tensor(B[0:64], ps[64:128, b, :], trig[0:64, 1, :], ALU.mult)
            return V.tensor_tensor(B[64:128], ps[0:64, b, :], trig[64:128, 1, :], ALU.mult)

        latent(0, range(4), C_QN)
        for t in range(TT):
            V.memset(y[:, t, :], 0.0).then_inc(y_zero, 1)
        dve.wait_ge(kr_ps, 1)
        link(rotate(1, None))
        V.tensor_tensor(scr[:, ROPE_A:ROPE_A + 512], scr[:, ROPE_A:ROPE_A + 512], scr[:, ROPE_B:ROPE_B + 512],
                        ALU.add).then_inc(kr_rot, 1)
        dve.wait_ge(kr_hi, 1)
        for par in (0, 1):
            for half in (0, 1):
                r0 = 64 * half + 32 * par
                op = V.tensor_tensor(krope[r0:r0 + 32, par, 1, :], scr[r0:r0 + 32, ROPE_A:ROPE_A + 512],
                                     krope[r0:r0 + 32, par, 0, :].bitcast(F32), ALU.subtract)
        op.then_inc(kr_lo, 1)
        dve.wait_ge(kr_lo, 1)
        latent(4, (4, 5, 6, 0), C_KVN)

        own_base = own[0]

        def pair(p):
            first = isinstance(p, int) and p == 0
            m0 = 8 + 2 * p

            def mine(op, k):
                op.then_inc(dve_own, 1)
                dve.wait_ge(dve_own, own_base + 5 * p + k)

            def proj_lo(k, dst, src, hi):
                dve.wait_ge(pj_hi, 7 * p + k + 1)
                V.tensor_tensor(dst, src, hi.bitcast(F32), ALU.subtract).then_inc(pj_lo, 1)

            dve.wait_ge(pj_ps, 7 * p + 1)
            mine(rotate(1, None), 1)
            V.tensor_tensor(scr[:, ROPE_A:ROPE_A + 512], scr[:, ROPE_A:ROPE_A + 512],
                            scr[:, ROPE_B:ROPE_B + 512], ALU.add).then_inc(q_rot, 1)
            ada_steps(m0, 0, 2)
            proj_lo(0, big[:, S_QR[1], :], scr[:, ROPE_A:ROPE_A + 512], big[:, S_QR[0], :])
            proj_lo(1, big[:, S_QN[1], :], ps[:, 0, :], big[:, S_QN[0], :])
            ada_steps(m0, 2, 4)
            proj_lo(2, big[:, S_QN[1] + 1, :], ps[:, 1, :], big[:, S_QN[0] + 1, :])
            ada_steps(m0, 4, 6)
            proj_lo(3, big[:, S_KN[1], :], ps[:, 0, :], big[:, S_KN[0], :])
            proj_lo(4, big[:, S_KN[1] + 1, :], ps[:, 1, :], big[:, S_KN[0] + 1, :])

            def maxima(hd):
                dve.wait_ge(s_ps, 2 * p + hd + 1)
                for i in range(TT):
                    b, o = S_AT[i]
                    op = V.reduce_max(stat[:, 8 + i:9 + i], ps[:, b, o:o + (i + 1) * P], AX_X)
                mine(op, 2 + 2 * hd)
                V.tensor_scalar(stat[:, 12:16], stat[:, 8:12], -SCALE, None, ALU.mult).then_inc(nbias, 1)

            def normed(hd):
                dve.wait_ge(s_exp, 2 * p + hd + 1)
                mine(V.reciprocal(stat[:, 20:24], stat[:, 16:20]), 3 + 2 * hd)
                for i in range(TT):
                    pr = scr[:, P_AT[i]:P_AT[i] + (i + 1) * P]
                    op = V.tensor_scalar(pr, pr, stat[:, 20 + i:21 + i], None, ALU.mult)
                op.then_inc(p_norm, 1)

            def turned_lo(hd):
                for n, i in enumerate(T_ORDER):
                    dve.wait_ge(t_hi, 8 * p + 4 * hd + max(n + 1, 2))
                    dst, hi = (big[:, s:s + i + 1, i * P:(i + 1) * P] for s in (S_PT[1], S_PT[0]))
                    b, o = t_at(i, hd)
                    src = ps[:, b, o:o + (i + 1) * P].rearrange("p (j c) -> p j c", c=P)
                    op = V.tensor_tensor(dst, src, hi.bitcast(F32), ALU.subtract)
                op.then_inc(t_lo, 1)

            def drains(n, steps):
                for t in range(TT):
                    if not first:
                        wo_add(p - 1, 4 * n + t)
                    ada_steps(m0, steps + t, steps + t + 1)

            maxima(0)
            ada_steps(m0, 6, 10)
            normed(0)
            for k, s in ((5, 0), (6, 2)):
                proj_lo(k, v_view(1)[:, s:s + 2], ps[:, k - 5, :].rearrange("p (t n) -> p t n", t=2),
                        v_view(0)[:, s:s + 2])
            drains(0, 10)
            turned_lo(0)
            ada_steps(m0, 14, 16)
            maxima(1)
            drains(1, 16)
            normed(1)
            dve.wait_ge(col_ps, 8 + 2 * p + 1)
            V.tensor_copy(sums[:, 0, bass.ds(4 * p, 4)], ps[:, 5, 0:4]).then_inc(col_saved, 1)
            drains(2, 20)
            turned_lo(1)
            drains(3, 24)
            ada_steps(m0, 28, 32)
            for hd in (0, 1):
                dve.wait_ge(ao_hi, 2 * p + hd + 1)
                V.tensor_tensor(big[:, S_AO[1] + hd, :], ps[:, (7, 4)[hd], :], big[:, S_AO[0] + hd, :].bitcast(F32),
                                ALU.subtract).then_inc(ao_lo, 1)
            dve.wait_ge(col_ps, 8 + 2 * p + 2)
            V.tensor_copy(sums[:, 1, bass.ds(4 * p, 4)], ps[:, 5, 0:4]).then_inc(col_saved, 1)

        def wo_add(q, m):
            n, t = divmod(m, TT)
            dst = y[:, t, n * 512:(n + 1) * 512]
            dve.wait_ge(wo_ps, 16 * q + m + 1)
            V.tensor_tensor(dst, dst, ps[:, m % 2, :], ALU.add).then_inc(wo_added, 1)

        pair(0)
        with dve.Fori(1, PAIRS) as p:
            pair(p)
        own[0] += 5 * PAIRS

        link(V.tensor_tensor(mod[:, 1, 0, :], sums[:, 0, 0:KT], pcol[:, C_B + 48:C_B + 48 + KT], ALU.add))
        link(V.tensor_tensor(mod[:, 1, 1, :], sums[:, 0, KT:], pcol[:, C_B + 64:C_B + 64 + KT], ALU.add))
        link(V.scalar_tensor_tensor(out=mod[:, 1, 1, :], in0=mod[:, 1, 1, :], scalar=1.0,
                                    in1=pcol[:, C_PRE + KT:C_PRE + 2 * KT], op0=ALU.add, op1=ALU.mult))
        for s in (0, 1):
            b0 = C_B + 48 * s + 32
            link(V.tensor_tensor(gate[:, s, :], sums[:, 1, s * KT:(s + 1) * KT], pcol[:, b0:b0 + KT], ALU.add))
            V.tensor_tensor(gate[:, s, :], gate[:, s, :], pcol[:, C_POST + s * KT:C_POST + (s + 1) * KT],
                            ALU.mult).then_inc(gate_done, 1)
        for m in range(4 * TT):
            wo_add(PAIRS - 1, m)

        def residual(t, n, k):
            row_rstd(n)
            if t == 0:
                dve.wait_ge(gate_full, 16 * (k + 1))
            link(V.scalar_tensor_tensor(out=y[:, t, :], in0=y[:, t, :], scalar=stat[:, 7:8], in1=ada[:, 0, :],
                                        op0=ALU.mult, op1=ALU.mult))
            dve.wait_ge(res_full[t % 2], 16 * (2 * k + t // 2 + 1))
            V.tensor_tensor(y[:, t, :], y[:, t, :], res_tile(t), ALU.add).then_inc(res_added, 1)

        def modulate(t):
            for g in range(4):
                n = 4 * t + g
                dve.wait_ge(xt_ps, KT + n + 1)
                if n >= 2:
                    dve.wait_ge(h_hi, KT + n - 1)
                for k in range(4 * g, 4 * g + 4):
                    o = (k % 4) * P
                    op = V.tensor_scalar(acc[:, n % 2, o:o + P], ps[:, 4 + g, o:o + P], mod[:, 1, 1, k:k + 1],
                                         mod[:, 1, 0, k:k + 1], ALU.mult, ALU.add)
                op.then_inc(mod_done, 1)
                dve.wait_ge(h_hi, KT + n + 1)
                V.tensor_tensor(big[:, 16 + 4 * g:20 + 4 * g, t * P:(t + 1) * P],
                                acc[:, n % 2, :].rearrange("p (k c) -> p k c", c=P),
                                big[:, 4 * g:4 * g + 4, t * P:(t + 1) * P].bitcast(F32),
                                ALU.subtract).then_inc(h_lo, 1)

        for t in range(TT):
            residual(t, TT + 2 * t, 0)
            row_rstd(TT + 2 * t + 1)
            V.tensor_scalar(res_tile(t), y[:, t, :], stat[:, 7:8], None, ALU.mult).then_inc(xn_done, 1)
            if t:
                modulate(t - 1)
        modulate(TT - 1)
        dve.wait_ge(x1_put, 16 * TT)
        for t in range(TT):
            V.memset(y[:, t, :], 0.0).then_inc(y_zero, 1)

        def mlp(c_):
            for j in range(4):
                n = 4 * c_ + j
                r = scr[:, (j % 2) * 512:(j % 2 + 1) * 512]
                s = scr[:, (2 + j % 2) * 512:(3 + j % 2) * 512]
                dve.wait_ge(act_relu, n + 1)
                V.tensor_tensor(s, r, r, ALU.mult).then_inc(act_sq, 1)
                dve.wait_ge(hid_hi, n + 1)
                dve.wait_ge(act_sq, n + 1)
                V.tensor_tensor(lat[:, 1, j, :], s, lat[:, 0, j, :].bitcast(F32),
                                ALU.subtract).then_inc(hid_lo, 1)
            for m in range(16):
                n, t = divmod(m, TT)
                dst = y[:, t, n * 512:(n + 1) * 512]
                dve.wait_ge(dn_ps, 16 * c_ + m + 1)
                V.tensor_tensor(dst, dst, ps[:, 4 + t, :], ALU.add).then_inc(dn_added, 1)

        with dve.Fori(0, CHUNKS) as c_:
            mlp(c_)
        for t in range(TT):
            residual(t, 3 * TT + t, 1)


    @block.tensor
    def _(pe):
        pe.wait_ge(par_full, 16 * 8)
        pe.wait_ge(consts, 7)
        nc.tensor.transpose(ps[:, 7, 0:N_B], scr[0:N_B, 0:P], ident[0:N_B, 0:N_B])
        n2 = N_PC - N_B
        nc.tensor.transpose(ps[:, 7, N_B:N_PC], scr[0:n2, P:2 * P], ident[0:n2, 0:n2]).then_inc(par_ps, 1)

        pe.wait_ge(xn_done, TT)
        for k in range(KT):
            if k >= 4:
                pe.wait_ge(xt_out, k - 3)
            for t in range(TT):
                op = nc.tensor.transpose(ps[:, k % 4, t * P:(t + 1) * P], y[:, t, k * P:(k + 1) * P], ident[:])
            op.then_inc(xt_ps, 1)

        def col_sum(chunk, which, b, o):
            pe.wait_ge(ada_step, 16 * (chunk + 1))
            for i in range(4):
                op = nc.tensor.matmul(ps[:, b, o + i:o + i + 1], acc[:, which, i * P:(i + 1) * P], ones[:, 0:1],
                                      start=True, stop=True)
            op.then_inc(col_ps, 1)

        pe.wait_ge(ones_done, 1)
        pe.wait_ge(par_cols, 1)
        for kk in range(4):
            if kk:
                pe.wait_ge(col_saved, 2 * kk)
            col_sum(2 * kk, 0, 7, 0)
            col_sum(2 * kk + 1, 1, 7, 4)
            if kk == 0:
                pe.wait_ge(xt_out, KT)
            for u, tiles in ((U_A[kk], range(0, 4)), (U_B[kk], range(4, 7))):
                pe.wait_ge(lo_done, u + 1)
                w = halves(u % 2, 4, 512 if tiles[0] == 0 else 384)
                for k in range(4):
                    if tiles[0] == 0:
                        pe.wait_ge(h_lo, 4 * kk + k + 1)
                    for j, b in enumerate(tiles):
                        if k < 3:
                            op = product(ps[:, b, :], [v[:, k, j * P:(j + 1) * P] for v in w], h_of(4 * kk + k),
                                         kk == 0 and k == 0, False)
                        else:
                            op = product(ps[:, b, :], [v[:, k, j * P:(j + 1) * P] for v in w], h_of(4 * kk + k),
                                         False, kk == 3)
                            if kk == 3:
                                op.then_inc(down_ps, 1)
                            elif j == len(tiles) - 1:
                                op.then_inc(unit_used, 1)

        def latent_sum(n0):
            for j in range(4):
                n = n0 + j
                pe.wait_ge(sq_done, n + 1)
                nc.tensor.matmul(ps[:, 7, :], ones[:], scr[:, (n % 2) * 512:(n % 2 + 1) * 512],
                                 start=(j == 0), stop=(j == 3)).then_inc(lat_sum, 1)

        pe.wait_ge(col_saved, 8)
        latent_sum(0)
        pe.wait_ge(lat_mul, 4)
        for i in (0, 1):
            pe.wait_ge(lo_done, U_C[i] + 1)
            w = halves(i, 8, 256)
            for part, b in ((0, 0), (1, 1)):
                for k in range(8):
                    op = product(ps[:, b, :], [v[:, k, part * P:(part + 1) * P] for v in w], h_of(8 * i + k),
                                 i == 0 and k == 0, i == 1 and k == 7)
                if i == 1:
                    op.then_inc(down_ps if part == 0 else kr_ps, 1)
                elif part == 1:
                    op.then_inc(unit_used, 1)
        pe.wait_ge(lat_var, 1)
        latent_sum(4)
        pe.wait_ge(kr_rot, 1)

        def wo_tile(q, m, w):
            n, t = divmod(m, TT)
            if m < 2:
                pe.wait_ge(pj_lo, 7 * (q + 1) + 6 + m if not (isinstance(q, int) and q == PAIRS - 1)
                           else 7 * PAIRS)
            if not (m < 2 and isinstance(q, int)):
                if m >= 2:
                    pe.wait_ge(wo_added, 16 * q + m - 1)
            if isinstance(q, int) and m < 2:
                pe.wait_ge(wo_added, 16 * q)
            for k in (0, 1):
                st = [big[:, S_AO[i] + k, t * P:(t + 1) * P] for i in (0, 1)]
                mv = [v[:, k, (n % 2) * 512:(n % 2 + 1) * 512] for v in w]
                op = product(ps[:, m % 2, :], st, mv, k == 0, k == 1)
            op.then_inc(wo_ps, 1)

        def pair(p):
            first = isinstance(p, int) and p == 0
            u = u_pair(p)
            wq = halves(0, 4, 2 * QD)
            wkv = halves(1, 4, 2 * KVD)

            def proj(k, b, w_cols, w, base):
                for kt in range(4):
                    op = product(ps[:, b, :], [w_cols(v[:, kt, :]) for v in w],
                                 (lat[:, 0, base + kt, :], lat[:, 1, base + kt, :]), kt == 0, kt == 3)
                op.then_inc(pj_ps, 1)
                return op

            pe.wait_ge(lo_done, u + 1)
            if first:
                pe.wait_ge(lat_lo, 4)
            else:
                pe.wait_ge(wo_added, 16 * (p - 1))
                pe.wait_ge(pj_lo, 7 * p)
            proj(0, 1, lambda v: v[:, 0:P], wq, 0)
            if first:
                pe.wait_ge(lat_lo, 8)
            proj(1, 0, lambda v: v[:, P:2 * P], wq, 0)
            pe.wait_ge(q_rot, p + 1)
            proj(2, 1, lambda v: v[:, 2 * P:3 * P], wq, 0)
            pe.wait_ge(lo_done, u + 2)
            pe.wait_ge(pj_lo, 7 * p + 2)
            proj(3, 0, lambda v: v[:, 0:NOPE], wkv, 4)
            pe.wait_ge(pj_lo, 7 * p + 3)
            proj(4, 1, lambda v: v[:, KVD:KVD + NOPE], wkv, 4)

            def scores(hd):
                pe.wait_ge(pj_lo, 7 * p + 4 + hd)
                if first and hd == 0:
                    pe.wait_ge(kr_lo, 1)
                if hd == 1:
                    pe.wait_ge(s_exp, 2 * p + 1)
                elif not first:
                    pe.wait_ge(s_exp, 2 * p)
                    pe.wait_ge(ao_lo, 2 * p)
                for i in range(TT):
                    b, o = S_AT[i]
                    ln = (i + 1) * P
                    q = slice(i * P, (i + 1) * P)
                    st = [big[:, s + hd, q] for s in S_QN]
                    mv = [big[:, s + hd, 0:ln] for s in S_KN]
                    product(ps[:, b, o:o + ln], st, mv, True, False)
                    nc.tensor.matmul(ps[:, b, o + i * P:o + ln], mask_u[:], mask_v[:], start=False, stop=False)
                    op = product(ps[:, b, o:o + ln], [big[:, s, q] for s in S_QR],
                                 [krope[:, hd, s, 0:ln] for s in (0, 1)], False, True)
                op.then_inc(s_ps, 1)

            def values():
                for t in range(TT):
                    b, o = t // 2, (t % 2) * 256
                    if t % 2 == 0:
                        pe.wait_ge(pj_lo, 7 * p + 4 + t // 2)
                    for kt in range(4):
                        st = [lat[:, i, 4 + kt, t * P:(t + 1) * P] for i in (0, 1)]
                        mv = [v[:, kt, :].rearrange("p (d n) -> p d n", d=2)[:, :, NOPE:] for v in wkv]
                        op = product(ps[:, b, o:o + 256], st, mv, kt == 0, kt == 3)
                    if t % 2 == 1:
                        op.then_inc(pj_ps, 1)

            def turn(hd):
                pe.wait_ge(p_norm, 2 * p + hd + 1)
                if hd == 1:
                    pe.wait_ge(t_lo, 2 * p + 1)
                    pe.wait_ge(col_saved, 8 + 2 * p + 1)
                elif not first:
                    pe.wait_ge(t_lo, 2 * p)
                    pe.wait_ge(col_saved, 8 + 2 * p)
                    pe.wait_ge(ao_lo, 2 * p)
                for i in T_ORDER:
                    b, o = t_at(i, hd)
                    for j in range(i + 1):
                        src = scr[:, P_AT[i] + j * P:P_AT[i] + (j + 1) * P]
                        op = nc.tensor.transpose(ps[:, b, o + j * P:o + (j + 1) * P], src, ident[:])
                op.then_inc(t_ps, 1)

            def weighted(hd):
                pe.wait_ge(t_lo, 2 * p + hd + 1)
                pe.wait_ge(pj_lo, 7 * p + 7)
                b = (7, 4)[hd]
                for j in range(TT):
                    st = [v_view(i)[:, j, hd * VDIM:(hd + 1) * VDIM] for i in (0, 1)]
                    mv = [big[:, S_PT[i] + j, j * P:TOK] for i in (0, 1)]
                    op = product(ps[:, b, j * P:TOK], st, mv, j == 0, j == TT - 1)
                op.then_inc(pv_ps, 1)

            def wo_block(n, w):
                for t in range(TT):
                    wo_tile(p - 1, 4 * n + t, w)

            wo = [halves(s, 2, 1024) for s in (0, 1)]
            scores(0)
            values()
            if not first:
                pe.wait_ge(lo_done, u + 3)
                pe.wait_ge(ao_lo, 2 * p)
                wo_block(0, wo[0])
            turn(0)
            scores(1)
            if not first:
                wo_block(1, wo[0])
            weighted(0)
            col_sum(8 + 2 * p, 0, 5, 0)
            if not first:
                pe.wait_ge(lo_done, u + 4)
                wo_block(2, wo[1])
            turn(1)
            if not first:
                wo_block(3, wo[1])
            weighted(1)
            col_sum(8 + 2 * p + 1, 1, 5, 0)

        pair(0)
        with pe.Fori(1, PAIRS) as p:
            pair(p)
        pe.wait_ge(ao_lo, 2 * PAIRS)
        for i in (0, 1):
            pe.wait_ge(lo_done, U_MLP - 2 + i + 1)
            w = halves(i, 2, 1024)
            for m in range(8 * i, 8 * i + 8):
                wo_tile(PAIRS - 1, m, w)

        for t in range(TT):
            pe.wait_ge(xn_done, TT + t + 1)
            for g in range(4):
                n = 4 * t + g
                if n >= 4:
                    pe.wait_ge(h_lo, KT + n - 3)
                else:
                    pe.wait_ge(ao_lo, 2 * PAIRS)
                    pe.wait_ge(col_saved, 8 + 2 * PAIRS)
                for k in range(4 * g, 4 * g + 4):
                    op = nc.tensor.transpose(ps[:, 4 + g, (k % 4) * P:(k % 4 + 1) * P],
                                             res_tile(t)[:, k * P:(k + 1) * P], ident[:])
                op.then_inc(xt_ps, 1)

        def mlp(c_):
            first = isinstance(c_, int)
            u = U_MLP + 8 * c_
            for kk in range(4):
                pe.wait_ge(lo_done, u + kk + 1)
                w = halves(kk % 2, 4, 512)
                if kk == 0 and not first:
                    pe.wait_ge(act_sq, 4 * c_)
                    pe.wait_ge(hid_hi, 4 * c_)
                for j in range(4):
                    for k in range(4):
                        op = product(ps[:, j, :], [v[:, k, j * P:(j + 1) * P] for v in w], h_of(4 * kk + k),
                                     kk == 0 and k == 0, kk == 3 and k == 3)
                    if kk == 3:
                        op.then_inc(up_ps, 1)
                if kk < 3:
                    op.then_inc(unit_used, 1)
            for n in range(4):
                pe.wait_ge(lo_done, u + 5 + n)
                w = halves(n % 2, 4, 512)
                order = ([(k, t) for k in range(4) for t in range(TT)] if n == 0 else
                         [(k, t) for t in range(TT) for k in range(4)])
                for k, t in order:
                    if n == 0 and t == 0:
                        pe.wait_ge(hid_lo, 4 * c_ + k + 1)
                    if k == 0 and not (first and n == 0):
                        pe.wait_ge(dn_added, 16 * c_ + 4 * n - 4 + t + 1)
                    st = [lat[:, i, k, t * P:(t + 1) * P] for i in (0, 1)]
                    op = product(ps[:, 4 + t, :], st, [v[:, k, :] for v in w], k == 0, k == 3)
                    if k == 3:
                        op.then_inc(dn_ps, 1)

        pe.wait_ge(h_lo, KT + 4 * TT)
        pe.wait_ge(sd_done, 3 * TT)
        mlp(0)
        with pe.Fori(1, CHUNKS) as c_:
            mlp(c_)

    ctx.close()


_INS = ["x", "c", "positions", "ada_w", "ada_b", "norm_pre", "norm_post", "mla_w_down", "mla_q_norm",
        "mla_w_uq", "mla_kv_norm", "mla_w_ukv", "mla_w_o", "mlp_up", "mlp_down"]


def kernel(**inputs):
    import numpy as _np
    import concourse.bacc as _bacc
    from concourse import mybir as _mybir
    from concourse.bass_utils import run_bass_kernel_spmd as _run

    nc = _bacc.Bacc("TRN2", target_bir_lowering=False, num_devices=1, dynamic_dma_scratch_size=1024)
    arrays, args = {}, []
    freq = _np.float32(10000.0) ** (-_np.arange(0, 64, 2, dtype=_np.float32) / _np.float32(64))
    consts = {"inv_freq": _np.tile(freq.astype(_np.float32), 4).reshape(128, 1)}
    for name in _INS + ["inv_freq"]:
        a = _np.ascontiguousarray(consts[name] if name in consts else inputs[name])
        arrays[f"in_{name}_dram"] = a
        args.append(nc.dram_tensor(f"in_{name}_dram", a.shape, _mybir.dt.from_np(a.dtype), kind="ExternalInput").ap())
    out = nc.dram_tensor("out_0_dram", (1, 512, 2048), _mybir.dt.float32, kind="ExternalOutput").ap()
    trunk(nc, *args, out)
    r = _run(nc, [arrays], core_ids=[0])
    return r.results[0]["out_0_dram"]
```

```python
from contextlib import ExitStack

import concourse.bass as bass
from concourse import mybir

F32 = mybir.dt.float32
F32R = mybir.dt.float32r
I32 = mybir.dt.int32
ALU = mybir.AluOpType
ACT = mybir.ActivationFunctionType
AX_X = mybir.AxisListType.X

P = 128
D = 2048
KT = D // P
TOK = 512
TT = TOK // P
LORA = 512
LT = LORA // P
HEADS = 16
NOPE = 128
ROPE = 64
HALF = ROPE // 2
VDIM = 128
QD = NOPE + ROPE
KVD = NOPE + VDIM
PAIRS = HEADS // 2
HIDDEN = 4 * D
CH = 512
CHUNKS = HIDDEN // CH
SCALE = float(QD) ** -0.5
EPS = 1e-6
MASKED = -1.0e30
ADA = 3 * D
Q_PARTS = 6
UNIT = 2048

U_A = [0, 2, 4, 6]
U_B = [1, 3, 5, 7]
U_C = [8, 9]
U_ATT = 10
U_MLP = 12 + 4 * (PAIRS - 1) + 2


def u_pair(p):
    return U_ATT if isinstance(p, int) and p == 0 else 8 + 4 * p


N_B = 2 * ADA // P
C_B = 0
C_C = N_B
C_PRE = C_C + KT
C_POST = C_PRE + 2 * KT
C_QN = C_POST + 2 * KT
C_KVN = C_QN + LT
N_PC = C_KVN + LT

S_QN, S_KN, S_QR, S_V, S_PT, S_AO = (0, 2), (4, 6), (8, 9), (10, 12), (14, 18), (22, 24)

S_AT = [(3, 384), (4, 0), (3, 0), (2, 0)]
P_AT = [0, 128, 384, 768]
ROPE_A, ROPE_B = 1280, 1792
T_ORDER = [2, 0, 1, 3]


def t_at(i, head):
    return [(6, 384), ((7, 4)[head], 0), (6, 0), (5, 0)][i]


def trunk(nc, x, c, positions, ada_w, ada_b, norm_pre, norm_post, w_down, q_norm, w_uq, kv_norm,
          w_ukv, w_o, mlp_up, mlp_down, inv_freq, out):
    ctx = ExitStack()

    def sb(name, shape, dt=F32):
        return ctx.enter_context(nc.sbuf_tensor(name, shape, dt))

    def sem(name):
        return ctx.enter_context(nc.semaphore(name))

    big = sb("big", [P, 32, 512], F32R)
    y = sb("y", [P, TT, D])
    lat = sb("lat", [P, 2, 8, 512], F32R)
    raw = sb("raw", [P, 2, UNIT])
    split = sb("split", [P, 2, 2, UNIT], F32R)
    ada = sb("ada", [P, 2, UNIT])
    scr = sb("scr", [P, 5 * 512])
    krope = sb("krope", [P, 2, 2, 512], F32R)
    trig = sb("trig", [P, 2, TOK])
    acc = sb("acc", [P, 2, 512])
    ident = sb("ident", [P, P])
    ones = sb("ones", [P, P])
    mask_u = sb("mask_u", [P, P], F32R)
    mask_v = sb("mask_v", [P, P], F32R)
    pcol = sb("pcol", [P, N_PC])
    csil = sb("csil", [P, 2, KT])
    mod = sb("mod", [P, 2, 2, KT])
    sums = sb("sums", [P, 2, 2 * KT])
    gate = sb("gate", [P, 2, KT])
    stat = sb("stat", [P, 32])
    ps = ctx.enter_context(nc.psum_tensor("ps", [P, 8, 512], F32))

    x1_dram = nc.dram_tensor("x1_scratch", [TOK, D], F32, kind="Internal").ap()
    gate_dram = nc.dram_tensor("gate_scratch", [2, D], F32, kind="Internal").ap()

    par_full = sem("par_full")
    x_full = [sem(f"x_full{t}") for t in range(TT)]
    q_full = sem("q_full")
    raw_full = [sem(f"raw_full{s}") for s in range(2)]
    ada_full = [sem(f"ada_full{s}") for s in range(3)]
    consts = sem("consts")
    ones_done = sem("ones_done")
    hi_done, lo_done, unit_used = sem("hi_done"), sem("lo_done"), sem("unit_used")
    ada_step = sem("ada_step")
    col_ps, col_saved = sem("col_ps"), sem("col_saved")
    par_ps, par_cols = sem("par_ps"), sem("par_cols")
    dve_own = sem("dve_own")
    c_exp = sem("c_exp")
    ss_done, var_done, sd_done, xn_done = sem("ss_done"), sem("var_done"), sem("sd_done"), sem("xn_done")
    xt_ps, xt_out = sem("xt_ps"), sem("xt_out")
    mod_done, h_hi, h_lo = sem("mod_done"), sem("h_hi"), sem("h_lo")
    down_ps, lat_out, sq_sum, lat_sum = (sem(n) for n in ("down_ps", "lat_out", "sq_sum", "lat_sum"))
    lat_var, lat_sd, lat_mul, lat_hi, lat_lo = (sem(n) for n in ("lat_var", "lat_sd", "lat_mul", "lat_hi", "lat_lo"))
    ang_done, trig_done = sem("ang_done"), sem("trig_done")
    kr_ps, kr_rot, kr_hi, kr_lo = sem("kr_ps"), sem("kr_rot"), sem("kr_hi"), sem("kr_lo")
    y_zero = sem("y_zero")
    pj_ps, pj_hi, pj_lo, q_rot = sem("pj_ps"), sem("pj_hi"), sem("pj_lo"), sem("q_rot")
    s_ps, s_max, nbias, s_exp, p_norm = (sem(n) for n in ("s_ps", "s_max", "nbias", "s_exp", "p_norm"))
    t_ps, t_hi, t_lo, pv_ps, ao_hi, ao_lo = (sem(n) for n in ("t_ps", "t_hi", "t_lo", "pv_ps", "ao_hi", "ao_lo"))
    wo_ps, wo_added = sem("wo_ps"), sem("wo_added")
    gate_done, gate_put, gate_full = sem("gate_done"), sem("gate_put"), sem("gate_full")
    res_full = [sem(f"res_full{s}") for s in range(2)]
    res_added, x1_put = sem("res_added"), sem("x1_put")
    up_ps, act_relu, act_sq, hid_hi, hid_lo = (sem(n) for n in ("up_ps", "act_relu", "act_sq", "hid_hi", "hid_lo"))
    dn_ps, dn_added = sem("dn_ps"), sem("dn_added")
    out_put = sem("out_put")

    x2 = x.rearrange("b s d -> (b s) d")
    out2 = out.rearrange("b s d -> (b s) d")
    w_dn, w_q, w_kv, w_out = w_down[0], w_uq[0], w_ukv[0], w_o[0]
    up, dn = mlp_up[0], mlp_down[0]
    xt_view = y[:].rearrange("p t (k c) -> p k t c", c=P)

    def rows(w, r0, n, c0, cols):
        return w[r0:r0 + n * P, c0:c0 + cols].rearrange("(k p) n -> p k n", p=P)

    def raw_of(u, n, cols):
        return raw[:, u % 2, :n * cols].rearrange("p (k n) -> p k n", k=n)

    def halves(s, n, cols):
        return [split[:, s, i, :n * cols].rearrange("p (k n) -> p k n", k=n) for i in (0, 1)]

    def product(o, st, mv, first, last):
        nc.tensor.matmul(o, st[0], mv[1], start=first, stop=False)
        nc.tensor.matmul(o, st[0], mv[0], start=False, stop=False)
        return nc.tensor.matmul(o, st[1], mv[0], start=False, stop=last)

    def h_of(k):
        return big[:, k, :], big[:, 16 + k, :]

    def res_tile(t):
        return ada[:, 1, :] if t % 2 == 0 else scr[:, 0:D]

    def ada_slot(s):
        return ada[:, s, :] if s < 2 else scr[:, 512:512 + UNIT]

    def c_parts(slot):
        r = raw[:, slot, :8 * 192].rearrange("p (k n) -> p k n", k=8)
        s = [split[:, slot, i, :].rearrange("p (k n) -> p k n", k=8) for i in (0, 1)]
        parts = [(r[:, :, 0:P], [s[0][:, :, 0:P], s[1][:, :, 0:P]])]
        r2 = r[:, :, P:192].rearrange("p k (h e) -> p k h e", h=2)
        s2 = [v[:, :, P:256].rearrange("p k (h d e) -> p k h d e", h=2, d=2) for v in s]
        for d in (0, 1):
            parts.append((r2, [v[:, :, :, d, :] for v in s2]))
        return parts

    def raw_count(u, slot):
        n = 8 * (u - slot) + 16
        if slot == 0 and not (isinstance(u, int) and u < U_ATT):
            n -= 16 * (PAIRS + 1)
        return n

    def lat_tile(n):
        return y[:, n // 4, (n % 4) * 512:(n % 4 + 1) * 512]

    def lat_square(n):
        return y[:, 2, n * 512:(n + 1) * 512] if n < 4 else ada[:, 1, (n - 4) * 512:(n - 3) * 512]

    def lat_row(i, j):
        return y[:, 3, (2 * i + j) * 512:(2 * i + j + 1) * 512]

    def v_view(i):
        return big[:, S_V[i]:S_V[i] + 2, :].rearrange("p s (t n) -> p (s t) n", t=2)

    block = ctx.enter_context(nc.Block())

    @block.sync
    def _(sp):
        def unit(u, src_list, slot, full=None):
            if not isinstance(u, int) or u >= 2:
                sp.wait_ge(lo_done, u - 1)
            for dst, src in src_list:
                sp.dma_start(dst, src).then_inc(full or raw_full[slot], 16)

        def ada_unit(m, slot, src, ring=2):
            if not isinstance(m, int):
                sp.wait_ge(ada_step, 4 * (m - 1))
            elif m == 2:
                sp.wait_ge(ang_done, 1)
            elif m >= ring:
                sp.wait_ge(ada_step, 4 * (m + 1 - ring))
            sp.dma_start(ada_slot(slot).rearrange("p (k n) -> p k n", k=4), src).then_inc(ada_full[slot], 16)

        b_rows = ada_b.rearrange("l s (r e) -> (l s r) e", e=P)
        sp.dma_start(scr[0:KT, P:2 * P], c.rearrange("b (r e) -> (b r) e", e=P)).then_inc(par_full, 16)
        sp.dma_start(scr[0:N_B, 0:P], b_rows).then_inc(par_full, 16)
        o = KT
        for a, n in ((norm_pre.rearrange("l s (r e) -> (l s r) e", e=P), 2 * KT),
                     (norm_post.rearrange("l s (r e) -> (l s r) e", e=P), 2 * KT),
                     (q_norm.rearrange("l (r e) -> (l r) e", e=P), LT),
                     (kv_norm.rearrange("l (r e) -> (l r) e", e=P), LT)):
            sp.dma_start(scr[o:o + n, P:2 * P], a).then_inc(par_full, 16)
            o += n
        sp.dma_start(stat[:, 0:1], inv_freq).then_inc(par_full, 16)
        sp.dma_start(scr[:, 512:1024].bitcast(I32), positions.broadcast_to([P, TOK])).then_inc(par_full, 16)
        for t in range(TT):
            sp.dma_start(y[:, t, :], x2[t * P:(t + 1) * P, :]).then_inc(x_full[t], 16)

        m = 0
        for kk in range(4):
            unit(U_A[kk], [(raw_of(0, 4, 512), rows(w_dn, kk * 512, 4, 0, 512))], 0)
            unit(U_B[kk], [(raw_of(1, 4, 384), rows(w_dn, kk * 512, 4, 512, 384))], 1)
            for part in (0, 1):
                for r in range(4):
                    ada_unit(m, m % 3, rows(ada_w[0, 0], r * 512, 4, part * D + kk * 512, 512), 3)
                    m += 1
        for i in (0, 1):
            unit(U_C[i], [(raw_of(i, 8, 192), rows(w_dn, i * 1024, 8, 896, 192))], i)

        def ada_two(p, a):
            for i in (0, 1):
                if a < 4:
                    src = ada_w[0, 1][(a + i) * 512:(a + i + 1) * 512, bass.ds(p * 512, 512)]
                else:
                    layer, col = p // (PAIRS // 2), 2 * D + (p % (PAIRS // 2)) * 512
                    src = ada_w[0][bass.ds(layer, 1), (a + i - 4) * 512:(a + i - 3) * 512, bass.ds(col, 512)]
                    src = src.rearrange("s r n -> (s r) n")
                ada_unit(32 + 8 * p + a + i, i, src.rearrange("(k p) n -> p k n", p=P))

        def pair_units(p, before=None):
            u = u_pair(p)
            first = isinstance(p, int) and p == 0
            q_src = w_q[:, bass.ds(p * (2 * QD), 2 * QD)].rearrange("(k p) n -> p k n", p=P)
            kv_col = 0 if first else (before * 2 + 2) * KVD
            kv_src = w_kv[:, bass.ds(kv_col, 2 * KVD)].rearrange("(k p) n -> p k n", p=P)
            q_dst = raw_of(0, 4, 2 * QD)
            parts = []
            for d in (0, 1):
                parts.append((q_dst[:, :, P * (1 + d):P * (2 + d)], q_src[:, :, QD * d:QD * d + NOPE]))
                for h in (0, 1):
                    o, i = HALF * (2 * h + d), QD * d + NOPE + HALF * h
                    parts.append((q_dst[:, :, o:o + HALF], q_src[:, :, i:i + HALF]))
            with nc.allow_non_contiguous_dma(reason="the rotary columns are runs of 128 bytes"):
                unit(u, parts, 0, q_full)
            if not first:
                ada_two(before, 6)
            unit(u + 1, [(raw_of(1, 4, 2 * KVD), kv_src)], 1)
            if first:
                sp.wait_ge(lat_lo, 8)
            ada_two(p, 0)
            if not first:
                o_rows = w_out[bass.ds(before * 256, 256), :].rearrange("(k p) n -> p k n", p=P)
                unit(u + 2, [(raw_of(0, 2, 1024), o_rows[:, :, 0:1024])], 0)
            ada_two(p, 2)
            if not first:
                unit(u + 3, [(raw_of(1, 2, 1024), o_rows[:, :, 1024:2048])], 1)
            ada_two(p, 4)

        pair_units(0)
        with sp.Fori(0, PAIRS - 1) as before:
            pair_units(before + 1, before)
        last = rows(w_out, (PAIRS - 1) * 256, 2, 0, D)
        cuts = [(k, a, b) for k in (0, 1) for a, b in ((0, 512), (512, 768), (768, 1024))]
        unit(U_MLP - 2, [(raw_of(0, 2, 1024)[:, k, a:b], last[:, k, a:b]) for k, a, b in cuts], 0, q_full)
        ada_two(PAIRS - 1, 6)
        unit(U_MLP - 1, [(raw_of(1, 2, 1024), last[:, :, 1024:])], 1)

        def gate_rows(s):
            sp.wait_ge(gate_done, s + 1)
            with nc.allow_non_contiguous_dma(reason="one word per partition and tile, 8 KB in all"):
                sp.dma_start(gate_dram[s].rearrange("(k p) -> p k", p=P), gate[:, s, :]).then_inc(gate_put, 16)
            sp.wait_ge(gate_put, 16 * (s + 1))
            sp.dma_start(ada[:, 0, :], gate_dram[s:s + 1, :].broadcast_to([P, D])).then_inc(gate_full, 16)

        def up_unit(c, kk):
            src = up[kk * 512:(kk + 1) * 512, bass.ds(c * CH, CH)]
            unit(U_MLP + 8 * c + kk, [(raw_of(kk, 4, 512), src.rearrange("(k p) n -> p k n", p=P))], kk % 2)

        def down_unit(c, n):
            src = dn[bass.ds(c * CH, CH), n * 512:(n + 1) * 512]
            unit(U_MLP + 8 * c + 4 + n, [(raw_of(n, 4, 512), src.rearrange("(k p) n -> p k n", p=P))], n % 2)

        gate_rows(0)
        up_unit(0, 0)
        up_unit(0, 1)
        sp.wait_ge(t_ps, 2 * PAIRS)
        for t in range(TT):
            if t >= 2:
                sp.wait_ge(xt_ps, KT + 4 * (t - 1))
            sp.dma_start(res_tile(t), x2[t * P:(t + 1) * P, :]).then_inc(res_full[t % 2], 16)
            if t >= 1:
                sp.wait_ge(res_added, t)
                sp.dma_start(x1_dram[(t - 1) * P:t * P, :], y[:, t - 1, :]).then_inc(x1_put, 16)
        sp.wait_ge(res_added, TT)
        sp.dma_start(x1_dram[(TT - 1) * P:, :], y[:, TT - 1, :]).then_inc(x1_put, 16)

        for kk in (2, 3):
            up_unit(0, kk)
        for n in range(4):
            down_unit(0, n)
        with sp.Fori(1, CHUNKS) as c_:
            for kk in range(4):
                up_unit(c_, kk)
            for n in range(4):
                down_unit(c_, n)
        sp.wait_ge(xt_ps, KT + 4 * TT)
        gate_rows(1)
        sp.wait_ge(x1_put, 16 * TT)
        sp.wait_ge(hid_lo, 4 * CHUNKS)
        for t in range(TT):
            if t >= 2:
                sp.wait_ge(res_added, TT + t - 1)
            sp.dma_start(res_tile(t), x1_dram[t * P:(t + 1) * P, :]).then_inc(res_full[t % 2], 16)
            if t >= 1:
                sp.wait_ge(res_added, TT + t)
                sp.dma_start(out2[(t - 1) * P:t * P, :], y[:, t - 1, :]).then_inc(out_put, 16)
        sp.wait_ge(res_added, 2 * TT)
        sp.dma_start(out2[(TT - 1) * P:, :], y[:, TT - 1, :]).then_inc(out_put, 16)
        sp.wait_ge(out_put, 16 * TT)


    @block.gpsimd
    def _(pool):
        G = nc.gpsimd
        nc.gpsimd.memset(ident[:], 0.0).then_inc(consts, 1)
        nc.gpsimd.memset(mask_u[:].bitcast(F32), 0.0).then_inc(consts, 1)
        nc.gpsimd.memset(mask_v[:].bitcast(F32), 0.0).then_inc(consts, 1)
        nc.gpsimd.memset(krope[:].bitcast(F32), 0.0).then_inc(consts, 1)
        pool.wait_ge(consts, 4)
        nc.gpsimd.affine_select(out=ident[:], in_=ident[:], compare_op=ALU.not_equal, fill=1.0, base=0,
                                pattern=[[-1, P]], channel_multiplier=1).then_inc(consts, 1)
        nc.gpsimd.memset(mask_u[0:1, 0:64].bitcast(F32), 1.0).then_inc(consts, 1)
        nc.gpsimd.memset(mask_v[0:1, 64:128].bitcast(F32), MASKED).then_inc(consts, 1)

        def lo(u, slot, words=UNIT):
            pool.wait_ge(hi_done, u + 1)
            nc.gpsimd.tensor_tensor(split[:, slot, 1, :words], raw[:, slot, :words],
                                    split[:, slot, 0, :words].bitcast(F32), ALU.subtract).then_inc(lo_done, 1)

        def lo_parts(u, parts):
            pool.wait_ge(hi_done, u + 1)
            for r, s in parts:
                op = nc.gpsimd.tensor_tensor(s[1], r, s[0].bitcast(F32), ALU.subtract)
            op.then_inc(lo_done, 1)

        for kk in range(4):
            lo(U_A[kk], 0)
            lo(U_B[kk], 1, 4 * 384)
            for k in range(4 * kk, 4 * kk + 4):
                pool.wait_ge(h_hi, k + 1)
                G.tensor_tensor(big[:, 16 + k, :].rearrange("p (t c) -> p t c", t=TT), xt_view[:, k],
                                big[:, k, :].bitcast(F32).rearrange("p (t c) -> p t c", t=TT),
                                ALU.subtract).then_inc(h_lo, 1)
        def latent_lo(i):
            for n in range(4 * i, 4 * i + 4):
                pool.wait_ge(lat_hi, n + 1)
                G.tensor_tensor(lat[:, 1, n, :], lat_square(n), lat[:, 0, n, :].bitcast(F32),
                                ALU.subtract).then_inc(lat_lo, 1)

        for u in (8, 9):
            lo_parts(u, c_parts(u % 2))
        latent_lo(0)
        lo(10, 0)
        lo(11, 1)
        latent_lo(1)
        pool.wait_ge(lat_lo, 8)
        for t in range(TT):
            G.memset(y[:, t, :], 0.0).then_inc(y_zero, 1)
        with pool.Fori(1, PAIRS) as p:
            for j in range(4):
                lo(u_pair(p) + j, j % 2)
        for j in (0, 1):
            lo(U_MLP - 2 + j, j)
        lo(U_MLP, 0)
        lo(U_MLP + 1, 1)
        pool.wait_ge(x1_put, 16 * TT)
        pool.wait_ge(xn_done, 2 * TT)
        for t in range(TT):
            G.memset(y[:, t, :], 0.0).then_inc(y_zero, 1)
        for j in range(2, 8):
            lo(U_MLP + j, j % 2)
        with pool.Fori(1, CHUNKS) as c_:
            for j in range(8):
                lo(U_MLP + 8 * c_ + j, j % 2)


    @block.scalar
    def _(act):
        def unit_hi(u, slot, used=None, count=None, parts=None, full=None, words=UNIT):
            act.wait_ge(*(full or (raw_full[slot], raw_count(u, slot))))
            if used is not None:
                act.wait_ge(used, count)
            for r, s in parts or [(raw[:, slot, :words], [split[:, slot, 0, :words]])]:
                op = nc.scalar.activation(s[0], r, ACT.Copy)
            op.then_inc(hi_done, 1)

        act.wait_ge(par_cols, 1)
        nc.scalar.activation(csil[:, 1, :], pcol[:, C_C:C_C + KT], ACT.Exp, scale=-1.0).then_inc(c_exp, 1)

        def row_stats(t, n, source):
            source(t)
            nc.scalar.activation(ps[:, 0:4, :].rearrange("p b n -> p (b n)"), y[:, t, :], ACT.Square,
                                 accum_out=stat[:, 4:5]).then_inc(ss_done, 1)
            act.wait_ge(var_done, n + 2 - TT)
            nc.scalar.activation(stat[:, 6:7], stat[:, 5:6], ACT.Sqrt).then_inc(sd_done, 1)

        for t in range(TT):
            act.wait_ge(x_full[t], 16)
            squares = big[:, 4 * t:4 * t + 4, :].rearrange("p s n -> p (s n)")
            nc.scalar.activation(squares, y[:, t, :], ACT.Square, accum_out=stat[:, 4 + t:5 + t]).then_inc(ss_done, 1)
        act.wait_ge(var_done, 1)
        nc.scalar.activation(stat[:, 12:16], stat[:, 8:12], ACT.Sqrt).then_inc(sd_done, 1)
        for k in range(KT):
            act.wait_ge(xt_ps, k + 1)
            nc.scalar.activation(xt_view[:, k], ps[:, k % 4, :].rearrange("p (t c) -> p t c", t=TT),
                                 ACT.Copy).then_inc(xt_out, 1)

        act.wait_ge(ang_done, 1)
        for i in (0, 1):
            nc.scalar.activation(trig[:, i, :], trig[:, i, :], ACT.Sin).then_inc(trig_done, 1)

        for kk in range(4):
            for u in (U_A[kk], U_B[kk]):
                words = 4 * 512 if u % 2 == 0 else 4 * 384
                if u < 2:
                    unit_hi(u, u % 2, words=words)
                else:
                    unit_hi(u, u % 2, unit_used, u - 1, words=words)
            for k in range(4 * kk, 4 * kk + 4):
                act.wait_ge(mod_done, k + 1)
                nc.scalar.activation(big[:, k, :].rearrange("p (t c) -> p t c", t=TT), xt_view[:, k],
                                     ACT.Copy).then_inc(h_hi, 1)

        def latent_out(n, b):
            act.wait_ge(down_ps, n + 1)
            nc.scalar.activation(lat_tile(n), ps[:, b, :], ACT.Copy)
            nc.scalar.activation(lat_square(n), ps[:, b, :], ACT.Square).then_inc(lat_out, 1)

        def latent_hi(i):
            act.wait_ge(lat_var, i + 1)
            nc.scalar.activation(lat_row(i, 0), lat_row(i, 0), ACT.Sqrt).then_inc(lat_sd, 1)
            for n in range(4 * i, 4 * i + 4):
                act.wait_ge(lat_mul, n + 1)
                nc.scalar.activation(lat[:, 0, n, :], lat_square(n), ACT.Copy).then_inc(lat_hi, 1)

        for n in range(4):
            latent_out(n, n)
        unit_hi(U_C[0], 0, down_ps, 4, c_parts(0))
        for n in range(4, 7):
            latent_out(n, n)
        unit_hi(U_C[1], 1, down_ps, 7, c_parts(1))
        latent_hi(0)
        unit_hi(10, 0, unit_used, 7, full=(q_full, 16 * Q_PARTS))
        latent_out(7, 0)
        act.wait_ge(kr_rot, 1)
        for par in (0, 1):
            for half in (0, 1):
                r0 = 64 * half + 32 * par
                op = nc.scalar.activation(krope[r0:r0 + 32, par, 0, :], scr[r0:r0 + 32, ROPE_A:ROPE_A + 512],
                                          ACT.Copy)
        op.then_inc(kr_hi, 1)
        unit_hi(11, 1, kr_ps, 1)
        latent_hi(1)

        def pair(p):
            first = isinstance(p, int) and p == 0
            u = u_pair(p)

            def proj_hi(k, dst, src):
                act.wait_ge(pj_ps, 7 * p + k + 1)
                nc.scalar.activation(dst, src, ACT.Copy).then_inc(pj_hi, 1)

            act.wait_ge(q_rot, p + 1)
            proj_hi(0, big[:, S_QR[0], :], scr[:, ROPE_A:ROPE_A + 512])
            proj_hi(1, big[:, S_QN[0], :], ps[:, 0, :])
            proj_hi(2, big[:, S_QN[0] + 1, :], ps[:, 1, :])
            proj_hi(3, big[:, S_KN[0], :], ps[:, 0, :])
            if not first:
                unit_hi(u + 2, 0, pj_ps, 7 * p + 3, full=(raw_full[0], 16 * (5 + p)))
            proj_hi(4, big[:, S_KN[0] + 1, :], ps[:, 1, :])

            def exps(hd):
                n = 2 * p + hd
                act.wait_ge(nbias, n + 1)
                if not (first and hd == 0):
                    act.wait_ge(t_ps, n)
                for i in range(TT):
                    b, o = S_AT[i]
                    ln = (i + 1) * P
                    op = nc.scalar.activation(scr[:, P_AT[i]:P_AT[i] + ln], ps[:, b, o:o + ln], ACT.Exp,
                                              bias=stat[:, 12 + i:13 + i], scale=SCALE,
                                              accum_out=stat[:, 16 + i:17 + i])
                op.then_inc(s_exp, 1)

            def turned_hi(hd):
                n = 2 * p + hd
                act.wait_ge(t_ps, n + 1)
                if not (first and hd == 0):
                    act.wait_ge(pv_ps, n)
                for i in T_ORDER:
                    dst = big[:, S_PT[0]:S_PT[0] + i + 1, i * P:(i + 1) * P]
                    b, o = t_at(i, hd)
                    src = ps[:, b, o:o + (i + 1) * P].rearrange("p (j c) -> p j c", c=P)
                    nc.scalar.activation(dst, src, ACT.Copy).then_inc(t_hi, 1)

            exps(0)
            proj_hi(5, v_view(0)[:, 0:2], ps[:, 0, :].rearrange("p (t n) -> p t n", t=2))
            proj_hi(6, v_view(0)[:, 2:4], ps[:, 1, :].rearrange("p (t n) -> p t n", t=2))
            if not first:
                unit_hi(u + 3, 1, pj_ps, 7 * p + 7)
            turned_hi(0)
            exps(1)
            if first:
                unit_hi(12, 0, pj_ps, 3, full=(q_full, 16 * Q_PARTS * 2))
            else:
                unit_hi(u + 4, 0, wo_ps, 16 * (p - 1) + 8, full=(q_full, 16 * Q_PARTS * (p + 2)))
            turned_hi(1)
            act.wait_ge(pv_ps, 2 * p + 2)
            for hd in (0, 1):
                nc.scalar.activation(big[:, S_AO[0] + hd, :], ps[:, (7, 4)[hd], :], ACT.Copy).then_inc(ao_hi, 1)
            if first:
                unit_hi(13, 1, pj_ps, 7)
            else:
                unit_hi(u + 5, 1, wo_ps, 16 * p)

        pair(0)
        with act.Fori(1, PAIRS) as p:
            pair(p)

        for i in (0, 1):
            unit_hi(U_MLP + i, i, wo_ps, 16 * (PAIRS - 1) + 8 * (i + 1))
        for tt in range(TT + 1):
            if tt < TT:
                row_stats(tt, TT + 2 * tt, lambda t: act.wait_ge(wo_added, 16 * PAIRS))
                row_stats(tt, TT + 2 * tt + 1, lambda t: act.wait_ge(res_added, t + 1))
            t = tt - 1
            for g in range(4) if t >= 0 else ():
                n = 4 * t + g
                act.wait_ge(mod_done, KT + n + 1)
                nc.scalar.activation(big[:, 4 * g:4 * g + 4, t * P:(t + 1) * P],
                                     acc[:, n % 2, :].rearrange("p (k c) -> p k c", c=P),
                                     ACT.Copy).then_inc(h_hi, 1)

        def mlp(c_):
            u = U_MLP + 8 * c_
            for j in range(2, 5):
                unit_hi(u + j, j % 2, unit_used, 7 + 3 * c_ + j - 1)
            for j in range(4):
                n = 4 * c_ + j
                act.wait_ge(up_ps, n + 1)
                if not (isinstance(c_, int) and j < 2):
                    act.wait_ge(act_sq, n - 1)
                nc.scalar.activation(scr[:, (j % 2) * 512:(j % 2 + 1) * 512], ps[:, j, :],
                                     ACT.Relu).then_inc(act_relu, 1)
                act.wait_ge(act_relu, n + 1)
                nc.scalar.activation(lat[:, 0, j, :], scr[:, (j % 2) * 512:(j % 2 + 1) * 512],
                                     ACT.Square).then_inc(hid_hi, 1)
            unit_hi(u + 5, 1, up_ps, 4 * c_ + 4)
            unit_hi(u + 6, 0, dn_ps, 16 * c_ + 4)
            unit_hi(u + 7, 1, dn_ps, 16 * c_ + 8)

        mlp(0)
        with act.Fori(1, CHUNKS) as c_:
            for j in (0, 1):
                unit_hi(U_MLP + 8 * c_ + j, j, dn_ps, 16 * (c_ - 1) + 12 + 4 * j)
            mlp(c_)
        for t in range(TT):
            row_stats(t, 3 * TT + t, lambda t: act.wait_ge(dn_added, 16 * CHUNKS))


    @block.vector
    def _(dve):
        own = [0]

        def link(op):
            own[0] += 1
            op.then_inc(dve_own, 1)
            dve.wait_ge(dve_own, own[0])

        V = nc.vector
        V.memset(ones[:], 1.0).then_inc(ones_done, 1)
        dve.wait_ge(par_ps, 1)
        V.tensor_copy(pcol[:], ps[:, 7, 0:N_PC]).then_inc(par_cols, 1)
        dve.wait_ge(c_exp, 1)
        link(V.tensor_scalar(csil[:, 1, :], csil[:, 1, :], 1.0, None, ALU.add))
        link(V.reciprocal(csil[:, 0, :], csil[:, 1, :]))
        link(V.tensor_tensor(csil[:, 0, :], pcol[:, C_C:C_C + KT], csil[:, 0, :], ALU.mult))

        turn, magic, edge = 6.283185307179586, 12582912.0, 3.1415925
        c1, c2 = 6.28125, 0.0019350051879882812
        ang, cnt, part = scr[:, 1024:1536], scr[:, 1536:2048], scr[:, 2048:2560]
        dve.wait_ge(par_full, 16 * 8)
        link(V.tensor_copy(ang, scr[:, 512:1024].bitcast(I32)))
        link(V.tensor_scalar(ang, ang, stat[:, 0:1], None, ALU.mult))
        for i, shift in ((0, 0.25), (1, 0.0)):
            to = trig[:, i, :]
            link(V.tensor_scalar(cnt, ang, 1.0 / turn, shift, ALU.mult, ALU.add))
            link(V.tensor_scalar(cnt, cnt, magic, None, ALU.add))
            link(V.tensor_scalar(cnt, cnt, -magic, None, ALU.add))
            for n, c in enumerate((c1, c2, turn - c1 - c2)):
                link(V.tensor_scalar(part, cnt, -c, None, ALU.mult))
                link(V.tensor_tensor(to, to if n else ang, part, ALU.add))
            link(V.tensor_scalar(to, to, shift * turn, None, ALU.add))
            link(V.tensor_scalar(to, to, edge, -edge, ALU.min, ALU.max))
        V.tensor_scalar(trig[0:64, 1, :], trig[0:64, 1, :], -1.0, None, ALU.mult).then_inc(ang_done, 1)

        def row_rstd(n):
            dve.wait_ge(ss_done, n + 1)
            V.tensor_scalar(stat[:, 5:6], stat[:, 4:5], 1.0 / D, EPS, ALU.mult, ALU.add).then_inc(var_done, 1)
            dve.wait_ge(sd_done, n + 2 - TT)
            link(V.reciprocal(stat[:, 7:8], stat[:, 6:7]))

        dve.wait_ge(ss_done, TT)
        V.tensor_scalar(stat[:, 8:12], stat[:, 4:8], 1.0 / D, EPS, ALU.mult, ALU.add).then_inc(var_done, 1)
        dve.wait_ge(sd_done, 1)
        link(V.reciprocal(stat[:, 16:20], stat[:, 12:16]))
        for t in range(TT):
            V.tensor_scalar(y[:, t, :], y[:, t, :], stat[:, 16 + t:17 + t], None, ALU.mult).then_inc(xn_done, 1)

        def ada_steps(chunk0, s0, s1):
            for s in range(s0, s1):
                k, row, which = s % 4, s % 16, s // 16
                if isinstance(chunk0, int) and chunk0 < 8:
                    m = 4 * chunk0 + s // 4
                    slot, full = m % 3, m // 3 + 1
                else:
                    slot, full = (s // 4) % 2, 2 * chunk0 - 16 + 11 + s // 8 + 1
                cols = ada_slot(slot)[:, k * 512:(k + 1) * 512]
                if k == 0:
                    dve.wait_ge(ada_full[slot], 16 * full)
                if row == 0:
                    if not (isinstance(chunk0, int) and chunk0 == 0):
                        dve.wait_ge(col_ps, chunk0 + which - 1)
                    op = V.tensor_scalar(acc[:, which, :], cols, csil[:, 0, 0:1], None, ALU.mult)
                else:
                    dve.wait_ge(ada_step, 16 * chunk0 + s)
                    op = V.scalar_tensor_tensor(out=acc[:, which, :], in0=cols, scalar=csil[:, 0, row:row + 1],
                                                in1=acc[:, which, :], op0=ALU.mult, op1=ALU.add)
                op.then_inc(ada_step, 1)

        for kk in range(4):
            cols = slice(4 * kk, 4 * kk + 4)
            ada_steps(2 * kk, 0, 32)
            dve.wait_ge(col_ps, 2 * kk + 2)
            V.tensor_tensor(mod[:, 0, 0, cols], ps[:, 7, 0:4], pcol[:, C_B + 4 * kk:C_B + 4 * kk + 4], ALU.add)
            link(V.tensor_tensor(mod[:, 0, 1, cols], ps[:, 7, 4:8],
                                 pcol[:, C_B + KT + 4 * kk:C_B + KT + 4 * kk + 4], ALU.add))
            V.scalar_tensor_tensor(out=mod[:, 0, 1, cols], in0=mod[:, 0, 1, cols], scalar=1.0,
                                   in1=pcol[:, C_PRE + 4 * kk:C_PRE + 4 * kk + 4], op0=ALU.add,
                                   op1=ALU.mult).then_inc(col_saved, 2)
            dve.wait_ge(col_saved, 2 * kk + 2)
            for k in range(4 * kk, 4 * kk + 4):
                dve.wait_ge(xt_out, k + 1)
                V.tensor_scalar(xt_view[:, k], xt_view[:, k], mod[:, 0, 1, k:k + 1], mod[:, 0, 0, k:k + 1],
                                ALU.mult, ALU.add).then_inc(mod_done, 1)

        def latent_square_sum(i):
            first = lat_square(4 * i)
            for n in range(4 * i + 1, 4 * i + 4):
                dve.wait_ge(lat_out, n + 1)
                op = V.tensor_tensor(first, first, lat_square(n), ALU.add)
                if n == 4 * i + 3:
                    op.then_inc(sq_sum, 1)
                else:
                    link(op)

        def latent(i, gcol):
            dve.wait_ge(lat_sum, i + 1)
            V.tensor_scalar(lat_row(i, 0), ps[:, 7, :], 1.0 / LORA, EPS, ALU.mult, ALU.add).then_inc(lat_var, 1)
            dve.wait_ge(lat_sd, i + 1)
            link(V.reciprocal(lat_row(i, 1), lat_row(i, 0)))
            for n in range(4 * i, 4 * i + 4):
                g = gcol + n - 4 * i
                V.scalar_tensor_tensor(out=lat_square(n), in0=lat_tile(n), scalar=pcol[:, g:g + 1],
                                       in1=lat_row(i, 1), op0=ALU.mult, op1=ALU.mult).then_inc(lat_mul, 1)

        def rotate(b, done):
            A, B = scr[:, ROPE_A:ROPE_A + 512], scr[:, ROPE_B:ROPE_B + 512]
            V.tensor_tensor(A, ps[:, b, :], trig[:, 0, :], ALU.mult)
            V.tensor_tensor(B[0:64], ps[64:128, b, :], trig[0:64, 1, :], ALU.mult)
            return V.tensor_tensor(B[64:128], ps[0:64, b, :], trig[64:128, 1, :], ALU.mult)

        latent_square_sum(0)
        latent(0, C_QN)
        dve.wait_ge(kr_ps, 1)
        dve.wait_ge(trig_done, 2)
        link(rotate(1, None))
        V.tensor_tensor(scr[:, ROPE_A:ROPE_A + 512], scr[:, ROPE_A:ROPE_A + 512], scr[:, ROPE_B:ROPE_B + 512],
                        ALU.add).then_inc(kr_rot, 1)
        latent_square_sum(1)
        dve.wait_ge(kr_hi, 1)
        for par in (0, 1):
            for half in (0, 1):
                r0 = 64 * half + 32 * par
                op = V.tensor_tensor(krope[r0:r0 + 32, par, 1, :], scr[r0:r0 + 32, ROPE_A:ROPE_A + 512],
                                     krope[r0:r0 + 32, par, 0, :].bitcast(F32), ALU.subtract)
        op.then_inc(kr_lo, 1)
        latent(1, C_KVN)

        own_base = own[0]

        def gate_sums(col, count):
            dve.wait_ge(col_ps, count)
            V.tensor_copy(sums[:, 1, bass.ds(col, 4)], ps[:, 5, 0:4]).then_inc(col_saved, 1)

        def pair(p):
            first = isinstance(p, int) and p == 0
            m0 = 8 + 2 * p

            def mine(op, k):
                op.then_inc(dve_own, 1)
                dve.wait_ge(dve_own, own_base + 5 * p + k)

            def proj_lo(k, dst, src, hi):
                dve.wait_ge(pj_hi, 7 * p + k + 1)
                V.tensor_tensor(dst, src, hi.bitcast(F32), ALU.subtract).then_inc(pj_lo, 1)

            dve.wait_ge(pj_ps, 7 * p + 1)
            mine(rotate(1, None), 1)
            V.tensor_tensor(scr[:, ROPE_A:ROPE_A + 512], scr[:, ROPE_A:ROPE_A + 512],
                            scr[:, ROPE_B:ROPE_B + 512], ALU.add).then_inc(q_rot, 1)
            ada_steps(m0, 0, 2)
            proj_lo(0, big[:, S_QR[1], :], scr[:, ROPE_A:ROPE_A + 512], big[:, S_QR[0], :])
            proj_lo(1, big[:, S_QN[1], :], ps[:, 0, :], big[:, S_QN[0], :])
            if not first:
                gate_sums(4 * p - 4, 8 + 2 * p)
            ada_steps(m0, 2, 4)
            proj_lo(2, big[:, S_QN[1] + 1, :], ps[:, 1, :], big[:, S_QN[0] + 1, :])
            proj_lo(3, big[:, S_KN[1], :], ps[:, 0, :], big[:, S_KN[0], :])
            proj_lo(4, big[:, S_KN[1] + 1, :], ps[:, 1, :], big[:, S_KN[0] + 1, :])

            def maxima(hd):
                dve.wait_ge(s_ps, 2 * p + hd + 1)
                for i in range(TT):
                    b, o = S_AT[i]
                    op = V.reduce_max(stat[:, 8 + i:9 + i], ps[:, b, o:o + (i + 1) * P], AX_X)
                mine(op, 2 + 2 * hd)
                V.tensor_scalar(stat[:, 12:16], stat[:, 8:12], -SCALE, None, ALU.mult).then_inc(nbias, 1)

            def normed(hd):
                dve.wait_ge(s_exp, 2 * p + hd + 1)
                mine(V.reciprocal(stat[:, 20:24], stat[:, 16:20]), 3 + 2 * hd)
                for i in range(TT):
                    pr = scr[:, P_AT[i]:P_AT[i] + (i + 1) * P]
                    op = V.tensor_scalar(pr, pr, stat[:, 20 + i:21 + i], None, ALU.mult)
                op.then_inc(p_norm, 1)

            def turned_lo(hd):
                for n, i in enumerate(T_ORDER):
                    dve.wait_ge(t_hi, 8 * p + 4 * hd + max(n + 1, 2))
                    dst, hi = (big[:, s:s + i + 1, i * P:(i + 1) * P] for s in (S_PT[1], S_PT[0]))
                    b, o = t_at(i, hd)
                    src = ps[:, b, o:o + (i + 1) * P].rearrange("p (j c) -> p j c", c=P)
                    op = V.tensor_tensor(dst, src, hi.bitcast(F32), ALU.subtract)
                op.then_inc(t_lo, 1)

            def drains(n, steps):
                for t in range(TT):
                    if not first:
                        wo_add(p - 1, 4 * n + t)
                    ada_steps(m0, steps + t, steps + t + 1)

            ada_steps(m0, 4, 6)
            maxima(0)
            ada_steps(m0, 6, 10)
            normed(0)
            for k, s in ((5, 0), (6, 2)):
                proj_lo(k, v_view(1)[:, s:s + 2], ps[:, k - 5, :].rearrange("p (t n) -> p t n", t=2),
                        v_view(0)[:, s:s + 2])
            drains(0, 10)
            turned_lo(0)
            ada_steps(m0, 14, 16)
            maxima(1)
            drains(1, 16)
            normed(1)
            dve.wait_ge(col_ps, 8 + 2 * p + 1)
            V.tensor_copy(sums[:, 0, bass.ds(4 * p, 4)], ps[:, 5, 0:4]).then_inc(col_saved, 1)
            drains(2, 20)
            turned_lo(1)
            drains(3, 24)
            ada_steps(m0, 28, 32)
            for hd in (0, 1):
                dve.wait_ge(ao_hi, 2 * p + hd + 1)
                V.tensor_tensor(big[:, S_AO[1] + hd, :], ps[:, (7, 4)[hd], :], big[:, S_AO[0] + hd, :].bitcast(F32),
                                ALU.subtract).then_inc(ao_lo, 1)

        def wo_add(q, m):
            n, t = divmod(m, TT)
            dst = y[:, t, n * 512:(n + 1) * 512]
            dve.wait_ge(wo_ps, 16 * q + m + 1)
            V.tensor_tensor(dst, dst, ps[:, m % 2, :], ALU.add).then_inc(wo_added, 1)

        pair(0)
        dve.wait_ge(y_zero, TT)
        with dve.Fori(1, PAIRS) as p:
            pair(p)
        own[0] += 5 * PAIRS
        gate_sums(4 * PAIRS - 4, 8 + 2 * PAIRS)

        dve.wait_ge(col_saved, 8 + 2 * PAIRS)
        link(V.tensor_tensor(mod[:, 1, 0, :], sums[:, 0, 0:KT], pcol[:, C_B + 48:C_B + 48 + KT], ALU.add))
        link(V.tensor_tensor(mod[:, 1, 1, :], sums[:, 0, KT:], pcol[:, C_B + 64:C_B + 64 + KT], ALU.add))
        link(V.scalar_tensor_tensor(out=mod[:, 1, 1, :], in0=mod[:, 1, 1, :], scalar=1.0,
                                    in1=pcol[:, C_PRE + KT:C_PRE + 2 * KT], op0=ALU.add, op1=ALU.mult))
        for s in (0, 1):
            b0 = C_B + 48 * s + 32
            link(V.tensor_tensor(gate[:, s, :], sums[:, 1, s * KT:(s + 1) * KT], pcol[:, b0:b0 + KT], ALU.add))
            V.tensor_tensor(gate[:, s, :], gate[:, s, :], pcol[:, C_POST + s * KT:C_POST + (s + 1) * KT],
                            ALU.mult).then_inc(gate_done, 1)
        for m in range(4 * TT):
            wo_add(PAIRS - 1, m)

        def residual(t, n, k):
            row_rstd(n)
            if t == 0:
                dve.wait_ge(gate_full, 16 * (k + 1))
            link(V.scalar_tensor_tensor(out=y[:, t, :], in0=y[:, t, :], scalar=stat[:, 7:8], in1=ada[:, 0, :],
                                        op0=ALU.mult, op1=ALU.mult))
            dve.wait_ge(res_full[t % 2], 16 * (2 * k + t // 2 + 1))
            V.tensor_tensor(y[:, t, :], y[:, t, :], res_tile(t), ALU.add).then_inc(res_added, 1)

        def modulate(t):
            for g in range(4):
                n = 4 * t + g
                dve.wait_ge(xt_ps, KT + n + 1)
                if n >= 2:
                    dve.wait_ge(h_hi, KT + n - 1)
                for k in range(4 * g, 4 * g + 4):
                    o = (k % 4) * P
                    op = V.tensor_scalar(acc[:, n % 2, o:o + P], ps[:, 4 + g, o:o + P], mod[:, 1, 1, k:k + 1],
                                         mod[:, 1, 0, k:k + 1], ALU.mult, ALU.add)
                op.then_inc(mod_done, 1)
                dve.wait_ge(h_hi, KT + n + 1)
                V.tensor_tensor(big[:, 16 + 4 * g:20 + 4 * g, t * P:(t + 1) * P],
                                acc[:, n % 2, :].rearrange("p (k c) -> p k c", c=P),
                                big[:, 4 * g:4 * g + 4, t * P:(t + 1) * P].bitcast(F32),
                                ALU.subtract).then_inc(h_lo, 1)

        for t in range(TT):
            residual(t, TT + 2 * t, 0)
            row_rstd(TT + 2 * t + 1)
            V.tensor_scalar(res_tile(t), y[:, t, :], stat[:, 7:8], None, ALU.mult).then_inc(xn_done, 1)
            if t:
                modulate(t - 1)
        modulate(TT - 1)
        dve.wait_ge(y_zero, 2 * TT)

        def mlp(c_):
            for j in range(4):
                n = 4 * c_ + j
                r = scr[:, (j % 2) * 512:(j % 2 + 1) * 512]
                s = scr[:, (2 + j % 2) * 512:(3 + j % 2) * 512]
                dve.wait_ge(act_relu, n + 1)
                V.tensor_tensor(s, r, r, ALU.mult).then_inc(act_sq, 1)
                dve.wait_ge(hid_hi, n + 1)
                dve.wait_ge(act_sq, n + 1)
                V.tensor_tensor(lat[:, 1, j, :], s, lat[:, 0, j, :].bitcast(F32),
                                ALU.subtract).then_inc(hid_lo, 1)
            for m in range(16):
                n, t = divmod(m, TT)
                dst = y[:, t, n * 512:(n + 1) * 512]
                dve.wait_ge(dn_ps, 16 * c_ + m + 1)
                V.tensor_tensor(dst, dst, ps[:, 4 + t, :], ALU.add).then_inc(dn_added, 1)

        with dve.Fori(0, CHUNKS) as c_:
            mlp(c_)
        for t in range(TT):
            residual(t, 3 * TT + t, 1)


    @block.tensor
    def _(pe):
        pe.wait_ge(par_full, 16 * 8)
        pe.wait_ge(consts, 7)
        nc.tensor.transpose(ps[:, 7, 0:N_B], scr[0:N_B, 0:P], ident[0:N_B, 0:N_B])
        n2 = N_PC - N_B
        nc.tensor.transpose(ps[:, 7, N_B:N_PC], scr[0:n2, P:2 * P], ident[0:n2, 0:n2]).then_inc(par_ps, 1)

        pe.wait_ge(xn_done, TT)
        for k in range(KT):
            if k >= 4:
                pe.wait_ge(xt_out, k - 3)
            for t in range(TT):
                op = nc.tensor.transpose(ps[:, k % 4, t * P:(t + 1) * P], y[:, t, k * P:(k + 1) * P], ident[:])
            op.then_inc(xt_ps, 1)

        def col_sum(chunk, which, b, o):
            pe.wait_ge(ada_step, 16 * (chunk + 1))
            for i in range(4):
                op = nc.tensor.matmul(ps[:, b, o + i:o + i + 1], acc[:, which, i * P:(i + 1) * P], ones[:, 0:1],
                                      start=True, stop=True)
            op.then_inc(col_ps, 1)

        pe.wait_ge(ones_done, 1)
        pe.wait_ge(par_cols, 1)
        for kk in range(4):
            if kk:
                pe.wait_ge(col_saved, 2 * kk)
            col_sum(2 * kk, 0, 7, 0)
            col_sum(2 * kk + 1, 1, 7, 4)
            if kk == 0:
                pe.wait_ge(xt_out, KT)
            for u, tiles in ((U_A[kk], range(0, 4)), (U_B[kk], range(4, 7))):
                pe.wait_ge(lo_done, u + 1)
                w = halves(u % 2, 4, 512 if tiles[0] == 0 else 384)
                for k in range(4):
                    if tiles[0] == 0:
                        pe.wait_ge(h_lo, 4 * kk + k + 1)
                    for j, b in enumerate(tiles):
                        if k < 3:
                            op = product(ps[:, b, :], [v[:, k, j * P:(j + 1) * P] for v in w], h_of(4 * kk + k),
                                         kk == 0 and k == 0, False)
                        else:
                            op = product(ps[:, b, :], [v[:, k, j * P:(j + 1) * P] for v in w], h_of(4 * kk + k),
                                         False, kk == 3)
                            if kk == 3:
                                op.then_inc(down_ps, 1)
                            elif j == len(tiles) - 1:
                                op.then_inc(unit_used, 1)

        def latent_sum(i):
            pe.wait_ge(sq_sum, i + 1)
            nc.tensor.matmul(ps[:, 7, :], ones[:], lat_square(4 * i), start=True, stop=True).then_inc(lat_sum, 1)

        pe.wait_ge(col_saved, 8)
        for i in (0, 1):
            pe.wait_ge(lo_done, U_C[i] + 1)
            w = halves(i, 8, 256)
            for part in (0, 1):
                if i == 0:
                    pe.wait_ge(lat_out, part + 1)
                for k in range(8):
                    op = product(ps[:, part, :], [v[:, k, part * P:(part + 1) * P] for v in w], h_of(8 * i + k),
                                 i == 0 and k == 0, i == 1 and k == 7)
                if i == 1:
                    op.then_inc(down_ps if part == 0 else kr_ps, 1)
                elif part == 1:
                    op.then_inc(unit_used, 1)
            if i == 1:
                pe.wait_ge(lat_var, 1)
            latent_sum(i)
        pe.wait_ge(kr_rot, 1)

        def wo_tile(q, m, w):
            n, t = divmod(m, TT)
            if m < 2:
                pe.wait_ge(pj_lo, 7 * (q + 1) + 6 + m if not (isinstance(q, int) and q == PAIRS - 1)
                           else 7 * PAIRS)
            if not (m < 2 and isinstance(q, int)):
                if m >= 2:
                    pe.wait_ge(wo_added, 16 * q + m - 1)
            if isinstance(q, int) and m < 2:
                pe.wait_ge(wo_added, 16 * q)
            for k in (0, 1):
                st = [big[:, S_AO[i] + k, t * P:(t + 1) * P] for i in (0, 1)]
                mv = [v[:, k, (n % 2) * 512:(n % 2 + 1) * 512] for v in w]
                op = product(ps[:, m % 2, :], st, mv, k == 0, k == 1)
            op.then_inc(wo_ps, 1)

        def pair(p):
            first = isinstance(p, int) and p == 0
            u = u_pair(p)
            wq = halves(0, 4, 2 * QD)
            wkv = halves(1, 4, 2 * KVD)

            def proj(k, b, w_cols, w, base):
                for kt in range(4):
                    op = product(ps[:, b, :], [w_cols(v[:, kt, :]) for v in w],
                                 (lat[:, 0, base + kt, :], lat[:, 1, base + kt, :]), kt == 0, kt == 3)
                op.then_inc(pj_ps, 1)
                return op

            pe.wait_ge(lo_done, u + 1)
            if first:
                pe.wait_ge(lat_lo, 4)
            else:
                pe.wait_ge(wo_added, 16 * (p - 1))
                pe.wait_ge(pj_lo, 7 * p)
            proj(0, 1, lambda v: v[:, 0:P], wq, 0)
            if first:
                pe.wait_ge(lat_out, 8)
            proj(1, 0, lambda v: v[:, P:2 * P], wq, 0)
            if not first:
                col_sum(7 + 2 * p, 1, 5, 0)
            pe.wait_ge(q_rot, p + 1)
            proj(2, 1, lambda v: v[:, 2 * P:3 * P], wq, 0)
            pe.wait_ge(lo_done, u + 2)
            pe.wait_ge(pj_lo, 7 * p + 2)
            if first:
                pe.wait_ge(lat_lo, 8)
            proj(3, 0, lambda v: v[:, 0:NOPE], wkv, 4)
            pe.wait_ge(pj_lo, 7 * p + 3)
            proj(4, 1, lambda v: v[:, KVD:KVD + NOPE], wkv, 4)

            def scores(hd):
                pe.wait_ge(pj_lo, 7 * p + 4 + hd)
                if first and hd == 0:
                    pe.wait_ge(kr_lo, 1)
                if hd == 1:
                    pe.wait_ge(s_exp, 2 * p + 1)
                elif not first:
                    pe.wait_ge(s_exp, 2 * p)
                    pe.wait_ge(ao_lo, 2 * p)
                for i in range(TT):
                    b, o = S_AT[i]
                    ln = (i + 1) * P
                    q = slice(i * P, (i + 1) * P)
                    st = [big[:, s + hd, q] for s in S_QN]
                    mv = [big[:, s + hd, 0:ln] for s in S_KN]
                    product(ps[:, b, o:o + ln], st, mv, True, False)
                    nc.tensor.matmul(ps[:, b, o + i * P:o + ln], mask_u[:], mask_v[:], start=False, stop=False)
                    op = product(ps[:, b, o:o + ln], [big[:, s, q] for s in S_QR],
                                 [krope[:, hd, s, 0:ln] for s in (0, 1)], False, True)
                op.then_inc(s_ps, 1)

            def values():
                for t in range(TT):
                    b, o = t // 2, (t % 2) * 256
                    if t % 2 == 0:
                        pe.wait_ge(pj_lo, 7 * p + 4 + t // 2)
                    for kt in range(4):
                        st = [lat[:, i, 4 + kt, t * P:(t + 1) * P] for i in (0, 1)]
                        mv = [v[:, kt, :].rearrange("p (d n) -> p d n", d=2)[:, :, NOPE:] for v in wkv]
                        op = product(ps[:, b, o:o + 256], st, mv, kt == 0, kt == 3)
                    if t % 2 == 1:
                        op.then_inc(pj_ps, 1)

            def turn(hd):
                pe.wait_ge(p_norm, 2 * p + hd + 1)
                if hd == 1:
                    pe.wait_ge(t_lo, 2 * p + 1)
                    pe.wait_ge(col_saved, 8 + 2 * p + 1)
                elif not first:
                    pe.wait_ge(t_lo, 2 * p)
                    pe.wait_ge(col_saved, 8 + 2 * p)
                    pe.wait_ge(ao_lo, 2 * p)
                for i in T_ORDER:
                    b, o = t_at(i, hd)
                    for j in range(i + 1):
                        src = scr[:, P_AT[i] + j * P:P_AT[i] + (j + 1) * P]
                        op = nc.tensor.transpose(ps[:, b, o + j * P:o + (j + 1) * P], src, ident[:])
                op.then_inc(t_ps, 1)

            def weighted(hd):
                pe.wait_ge(t_lo, 2 * p + hd + 1)
                pe.wait_ge(pj_lo, 7 * p + 7)
                b = (7, 4)[hd]
                for j in range(TT):
                    st = [v_view(i)[:, j, hd * VDIM:(hd + 1) * VDIM] for i in (0, 1)]
                    mv = [big[:, S_PT[i] + j, j * P:TOK] for i in (0, 1)]
                    op = product(ps[:, b, j * P:TOK], st, mv, j == 0, j == TT - 1)
                op.then_inc(pv_ps, 1)

            def wo_block(n, w):
                for t in range(TT):
                    wo_tile(p - 1, 4 * n + t, w)

            wo = [halves(s, 2, 1024) for s in (0, 1)]
            scores(0)
            values()
            if not first:
                pe.wait_ge(lo_done, u + 3)
                pe.wait_ge(ao_lo, 2 * p)
                wo_block(0, wo[0])
            turn(0)
            scores(1)
            if not first:
                wo_block(1, wo[0])
            weighted(0)
            col_sum(8 + 2 * p, 0, 5, 0)
            if not first:
                pe.wait_ge(lo_done, u + 4)
                wo_block(2, wo[1])
            turn(1)
            if not first:
                wo_block(3, wo[1])
            weighted(1)

        pair(0)
        with pe.Fori(1, PAIRS) as p:
            pair(p)
        col_sum(7 + 2 * PAIRS, 1, 5, 0)
        pe.wait_ge(ao_lo, 2 * PAIRS)
        for i in (0, 1):
            pe.wait_ge(lo_done, U_MLP - 2 + i + 1)
            w = halves(i, 2, 1024)
            for m in range(8 * i, 8 * i + 8):
                wo_tile(PAIRS - 1, m, w)

        for t in range(TT):
            pe.wait_ge(xn_done, TT + t + 1)
            for g in range(4):
                n = 4 * t + g
                if n >= 4:
                    pe.wait_ge(h_lo, KT + n - 3)
                else:
                    pe.wait_ge(ao_lo, 2 * PAIRS)
                    pe.wait_ge(col_saved, 8 + 2 * PAIRS)
                for k in range(4 * g, 4 * g + 4):
                    op = nc.tensor.transpose(ps[:, 4 + g, (k % 4) * P:(k % 4 + 1) * P],
                                             res_tile(t)[:, k * P:(k + 1) * P], ident[:])
                op.then_inc(xt_ps, 1)

        def mlp(c_):
            first = isinstance(c_, int)
            u = U_MLP + 8 * c_
            for kk in range(4):
                pe.wait_ge(lo_done, u + kk + 1)
                w = halves(kk % 2, 4, 512)
                if kk == 0 and not first:
                    pe.wait_ge(act_sq, 4 * c_)
                    pe.wait_ge(hid_hi, 4 * c_)
                for j in range(4):
                    for k in range(4):
                        op = product(ps[:, j, :], [v[:, k, j * P:(j + 1) * P] for v in w], h_of(4 * kk + k),
                                     kk == 0 and k == 0, kk == 3 and k == 3)
                    if kk == 3:
                        op.then_inc(up_ps, 1)
                if kk < 3:
                    op.then_inc(unit_used, 1)
            for n in range(4):
                pe.wait_ge(lo_done, u + 5 + n)
                w = halves(n % 2, 4, 512)
                order = ([(k, t) for k in range(4) for t in range(TT)] if n == 0 else
                         [(k, t) for t in range(TT) for k in range(4)])
                for k, t in order:
                    if n == 0 and t == 0:
                        pe.wait_ge(hid_lo, 4 * c_ + k + 1)
                    if k == 0 and not (first and n == 0):
                        pe.wait_ge(dn_added, 16 * c_ + 4 * n - 4 + t + 1)
                    st = [lat[:, i, k, t * P:(t + 1) * P] for i in (0, 1)]
                    op = product(ps[:, 4 + t, :], st, [v[:, k, :] for v in w], k == 0, k == 3)
                    if k == 3:
                        op.then_inc(dn_ps, 1)

        pe.wait_ge(h_lo, KT + 4 * TT)
        pe.wait_ge(sd_done, 2 * TT + 1)
        mlp(0)
        with pe.Fori(1, CHUNKS) as c_:
            mlp(c_)

    ctx.close()


_INS = ["x", "c", "positions", "ada_w", "ada_b", "norm_pre", "norm_post", "mla_w_down", "mla_q_norm",
        "mla_w_uq", "mla_kv_norm", "mla_w_ukv", "mla_w_o", "mlp_up", "mlp_down"]


def kernel(**inputs):
    import numpy as _np
    import concourse.bacc as _bacc
    from concourse import mybir as _mybir
    from concourse.bass_utils import run_bass_kernel_spmd as _run

    nc = _bacc.Bacc("TRN2", target_bir_lowering=False, num_devices=1, dynamic_dma_scratch_size=1024)
    arrays, args = {}, []
    freq = _np.float32(10000.0) ** (-_np.arange(0, 64, 2, dtype=_np.float32) / _np.float32(64))
    consts = {"inv_freq": _np.tile(freq.astype(_np.float32), 4).reshape(128, 1)}
    for name in _INS + ["inv_freq"]:
        a = _np.ascontiguousarray(consts[name] if name in consts else inputs[name])
        arrays[f"in_{name}_dram"] = a
        args.append(nc.dram_tensor(f"in_{name}_dram", a.shape, _mybir.dt.from_np(a.dtype), kind="ExternalInput").ap())
    out = nc.dram_tensor("out_0_dram", (1, 512, 2048), _mybir.dt.float32, kind="ExternalOutput").ap()
    trunk(nc, *args, out)
    r = _run(nc, [arrays], core_ids=[0])
    return r.results[0]["out_0_dram"]
```

```python
from contextlib import ExitStack

import concourse.bass as bass
from concourse import mybir

F32 = mybir.dt.float32
F32R = mybir.dt.float32r
I32 = mybir.dt.int32
ALU = mybir.AluOpType
ACT = mybir.ActivationFunctionType
AX_X = mybir.AxisListType.X

P = 128
D = 2048
KT = D // P
TOK = 512
TT = TOK // P
LORA = 512
LT = LORA // P
HEADS = 16
NOPE = 128
ROPE = 64
HALF = ROPE // 2
VDIM = 128
QD = NOPE + ROPE
KVD = NOPE + VDIM
PAIRS = HEADS // 2
HIDDEN = 4 * D
CH = 512
CHUNKS = HIDDEN // CH
SCALE = float(QD) ** -0.5
EPS = 1e-6
MASKED = -1.0e30
ADA = 3 * D
Q_PARTS = 6
UNIT = 2048

U_A = [0, 2, 4, 6]
U_B = [1, 3, 5, 7]
U_C = [8, 9]
U_ATT = 10
U_MLP = 12 + 4 * (PAIRS - 1) + 2


def u_pair(p):
    return U_ATT if isinstance(p, int) and p == 0 else 8 + 4 * p


N_B = 2 * ADA // P
C_B = 0
C_C = N_B
C_PRE = C_C + KT
C_POST = C_PRE + 2 * KT
C_QN = C_POST + 2 * KT
C_KVN = C_QN + LT
N_PC = C_KVN + LT

S_QN, S_KN, S_QR, S_V, S_PT, S_AO = (0, 2), (4, 6), (8, 9), (10, 12), (14, 18), (22, 24)

S_AT = [(3, 384), (4, 0), (3, 0), (2, 0)]
P_AT = [0, 128, 384, 768]
ROPE_A, ROPE_B = 1280, 1792
LAST_WO = [(0, 0), (0, 1), (1, 0), (1, 1), (0, 2), (0, 3), (1, 2), (1, 3)] + [(t, n) for t in (2, 3) for n in range(4)]
T_ORDER = [2, 0, 1, 3]


def t_at(i, head):
    return [(6, 384), ((7, 4)[head], 0), (6, 0), (5, 0)][i]


def trunk(nc, x, c, positions, ada_w, ada_b, norm_pre, norm_post, w_down, q_norm, w_uq, kv_norm,
          w_ukv, w_o, mlp_up, mlp_down, inv_freq, out):
    ctx = ExitStack()

    def sb(name, shape, dt=F32):
        return ctx.enter_context(nc.sbuf_tensor(name, shape, dt))

    def sem(name):
        return ctx.enter_context(nc.semaphore(name))

    big = sb("big", [P, 32, 512], F32R)
    y = sb("y", [P, TT, D])
    lat = sb("lat", [P, 2, 8, 512], F32R)
    raw = sb("raw", [P, 2, UNIT])
    split = sb("split", [P, 2, 2, UNIT], F32R)
    ada = sb("ada", [P, 2, UNIT])
    scr = sb("scr", [P, 5 * 512])
    krope = sb("krope", [P, 2, 2, 512], F32R)
    trig = sb("trig", [P, 2, TOK])
    acc = sb("acc", [P, 2, 512])
    ident = sb("ident", [P, P])
    ones = sb("ones", [P, P])
    mask_u = sb("mask_u", [P, P], F32R)
    mask_v = sb("mask_v", [P, P], F32R)
    pcol = sb("pcol", [P, N_PC])
    csil = sb("csil", [P, 2, KT])
    mod = sb("mod", [P, 2, KT])
    sums = sb("sums", [P, 2, 2 * KT])
    four = sb("four", [P, 4, KT])
    stat = sb("stat", [P, 96])
    ps = ctx.enter_context(nc.psum_tensor("ps", [P, 8, 512], F32))

    x1_dram = nc.dram_tensor("x1_scratch", [TOK, D], F32, kind="Internal").ap()
    row_dram = nc.dram_tensor("row_scratch", [4, D], F32, kind="Internal").ap()

    par_full = sem("par_full")
    x_full = [sem(f"x_full{t}") for t in range(TT)]
    q_full = sem("q_full")
    raw_full = [sem(f"raw_full{s}") for s in range(2)]
    ada_full = [sem(f"ada_full{s}") for s in range(3)]
    consts = sem("consts")
    ones_done = sem("ones_done")
    hi_done, lo_done, unit_used = sem("hi_done"), sem("lo_done"), sem("unit_used")
    ada_step = sem("ada_step")
    col_ps, col_saved = sem("col_ps"), sem("col_saved")
    par_ps, par_cols = sem("par_ps"), sem("par_cols")
    dve_own = sem("dve_own")
    c_exp = sem("c_exp")
    ss_done, var_done, sd_done, xn_done = sem("ss_done"), sem("var_done"), sem("sd_done"), sem("xn_done")
    xt_ps, xt_out = sem("xt_ps"), sem("xt_out")
    mod_done, h_hi, h_lo = sem("mod_done"), sem("h_hi"), sem("h_lo")
    down_ps, lat_out, sq_sum, lat_sum = (sem(n) for n in ("down_ps", "lat_out", "sq_sum", "lat_sum"))
    lat_var, lat_sd, lat_mul, lat_hi, lat_lo = (sem(n) for n in ("lat_var", "lat_sd", "lat_mul", "lat_hi", "lat_lo"))
    ang_done, trig_done = sem("ang_done"), sem("trig_done")
    kv_lo = sem("kv_lo")
    kr_ps, kr_rot, kr_hi, kr_lo = sem("kr_ps"), sem("kr_rot"), sem("kr_hi"), sem("kr_lo")
    y_zero = sem("y_zero")
    pj_ps, pj_hi, pj_lo, q_rot = sem("pj_ps"), sem("pj_hi"), sem("pj_lo"), sem("q_rot")
    s_ps, nbias, s_exp, p_norm = (sem(n) for n in ("s_ps", "nbias", "s_exp", "p_norm"))
    t_ps, t_hi, t_lo, pv_ps, ao_hi, ao_lo = (sem(n) for n in ("t_ps", "t_hi", "t_lo", "pv_ps", "ao_hi", "ao_lo"))
    wo_ps, wo_added = sem("wo_ps"), sem("wo_added")
    four_done, four_ps, four_out, four_put = (sem(n) for n in ("four_done", "four_ps", "four_out", "four_put"))
    row_full = [sem(f"row_full{i}") for i in range(4)]
    res_full = [sem(f"res_full{s}") for s in range(2)]
    res_mul, h_mul = sem("res_mul"), sem("h_mul")
    res_added = [sem(f"res_added{t}") for t in range(TT)]
    x1_put = [sem(f"x1_put{t}") for t in range(TT)]
    x1_full = [sem(f"x1_full{t}") for t in range(TT)]
    up_ps, act_relu, act_sq, hid_hi, hid_lo = (sem(n) for n in ("up_ps", "act_relu", "act_sq", "hid_hi", "hid_lo"))
    dn_ps, dn_added = sem("dn_ps"), sem("dn_added")
    blk_sq, blk_gate, last_gate = sem("blk_sq"), sem("blk_gate"), sem("last_gate")
    out_done, out_put = sem("out_done"), sem("out_put")

    x2 = x.rearrange("b s d -> (b s) d")
    out2 = out.rearrange("b s d -> (b s) d")
    w_dn, w_q, w_kv, w_out = w_down[0], w_uq[0], w_ukv[0], w_o[0]
    up, dn = mlp_up[0], mlp_down[0]
    xt_view = y[:].rearrange("p t (k c) -> p k t c", c=P)

    def rows(w, r0, n, c0, cols):
        return w[r0:r0 + n * P, c0:c0 + cols].rearrange("(k p) n -> p k n", p=P)

    def raw_of(u, n, cols):
        return raw[:, u % 2, :n * cols].rearrange("p (k n) -> p k n", k=n)

    def halves(s, n, cols):
        return [split[:, s, i, :n * cols].rearrange("p (k n) -> p k n", k=n) for i in (0, 1)]

    def product(o, st, mv, first, last):
        nc.tensor.matmul(o, st[0], mv[1], start=first, stop=False)
        nc.tensor.matmul(o, st[0], mv[0], start=False, stop=False)
        return nc.tensor.matmul(o, st[1], mv[0], start=False, stop=last)

    def h_of(k):
        return big[:, k, :], big[:, 16 + k, :]

    def res_tile(t):
        return ada[:, 1, :] if t % 2 == 0 else scr[:, 0:D]

    row_at = {0: ada[:, 0, :], 1: lat[:, 0, 0:4, :].rearrange("p k n -> p (k n)").bitcast(F32), 3: ada[:, 0, :]}

    STATS = [(1, 0), (1, 1), (1, 2), (2, 0), (1, 3), (2, 1), (2, 2), (2, 3)] + [(3, t) for t in range(TT)]

    def stat_cols(stage, t):
        q = STATS.index((stage, t))
        return [stat[:, 32 + 16 * i + q:33 + 16 * i + q] for i in range(3)]

    def turn_bank(t):
        return 0 if t == 1 else 4

    def x1_again(t):
        return big[:, 4 * t:4 * t + 4, :].rearrange("p k n -> p (k n)").bitcast(F32)

    def ada_slot(s):
        return ada[:, s, :] if s < 2 else scr[:, 512:512 + UNIT]

    def c_parts(slot):
        r = raw[:, slot, :8 * 192].rearrange("p (k n) -> p k n", k=8)
        s = [split[:, slot, i, :].rearrange("p (k n) -> p k n", k=8) for i in (0, 1)]
        parts = [(r[:, :, 0:P], [s[0][:, :, 0:P], s[1][:, :, 0:P]])]
        r2 = r[:, :, P:192].rearrange("p k (h e) -> p k h e", h=2)
        s2 = [v[:, :, P:256].rearrange("p k (h d e) -> p k h d e", h=2, d=2) for v in s]
        for d in (0, 1):
            parts.append((r2, [v[:, :, :, d, :] for v in s2]))
        return parts

    def raw_count(u, slot):
        n = 8 * (u - slot) + 16
        if slot == 0 and not (isinstance(u, int) and u < U_ATT):
            n -= 16 * (PAIRS + 1)
        return n

    def lat_tile(n):
        return y[:, n // 4, (n % 4) * 512:(n % 4 + 1) * 512]

    def lat_square(n):
        return y[:, 2, n * 512:(n + 1) * 512] if n < 4 else ada[:, 1, (n - 4) * 512:(n - 3) * 512]

    def lat_row(i, j):
        return y[:, 3, (2 * i + j) * 512:(2 * i + j + 1) * 512]

    def v_view(i):
        return big[:, S_V[i]:S_V[i] + 2, :].rearrange("p s (t n) -> p (s t) n", t=2)

    eps_col = stat[:, 31:32]
    block = ctx.enter_context(nc.Block())

    @block.sync
    def _(sp):
        def unit(u, src_list, slot, full=None):
            if not isinstance(u, int) or u >= 2:
                sp.wait_ge(lo_done, u - 1)
            for dst, src in src_list:
                sp.dma_start(dst, src).then_inc(full or raw_full[slot], 16)

        def ada_unit(m, slot, src, ring=2):
            if not isinstance(m, int):
                sp.wait_ge(ada_step, 4 * (m - 1))
            elif m == 2:
                sp.wait_ge(ang_done, 1)
            elif m >= ring:
                sp.wait_ge(ada_step, 4 * (m + 1 - ring))
            dst = ada_slot(slot).rearrange("p (k n) -> p k n", k=4)
            w = 512 // len(src)
            for i, part in enumerate(src):
                sp.dma_start(dst[:, :, i * w:(i + 1) * w], part).then_inc(ada_full[slot], 16)

        b_rows = ada_b.rearrange("l s (r e) -> (l s r) e", e=P)
        sp.dma_start(scr[0:KT, P:2 * P], c.rearrange("b (r e) -> (b r) e", e=P)).then_inc(par_full, 16)
        sp.dma_start(scr[0:N_B, 0:P], b_rows).then_inc(par_full, 16)
        o = KT
        for a, n in ((norm_pre.rearrange("l s (r e) -> (l s r) e", e=P), 2 * KT),
                     (norm_post.rearrange("l s (r e) -> (l s r) e", e=P), 2 * KT),
                     (q_norm.rearrange("l (r e) -> (l r) e", e=P), LT),
                     (kv_norm.rearrange("l (r e) -> (l r) e", e=P), LT)):
            sp.dma_start(scr[o:o + n, P:2 * P], a).then_inc(par_full, 16)
            o += n
        sp.dma_start(stat[:, 0:1], inv_freq).then_inc(par_full, 16)
        sp.dma_start(scr[:, 512:1024].bitcast(I32), positions.broadcast_to([P, TOK])).then_inc(par_full, 16)
        for t in range(TT):
            sp.dma_start(y[:, t, :], x2[t * P:(t + 1) * P, :]).then_inc(x_full[t], 16)

        m = 0
        for kk in range(4):
            unit(U_A[kk], [(raw_of(0, 4, 512), rows(w_dn, kk * 512, 4, 0, 512))], 0)
            unit(U_B[kk], [(raw_of(1, 4, 384), rows(w_dn, kk * 512, 4, 512, 384))], 1)
            for i in range(8):
                if kk < 3:
                    part, r, cols = i // 4, i % 4, kk * 512
                    src = [rows(ada_w[0, 0], r * 512, 4, part * D + cols, 512)]
                else:
                    r, cols = i % 4, kk * 512 + (i // 4) * 256
                    src = [rows(ada_w[0, 0], r * 512, 4, part * D + cols, 256) for part in (0, 1)]
                ada_unit(m, m % 3, src, 3)
                m += 1
        for i in (0, 1):
            unit(U_C[i], [(raw_of(i, 8, 192), rows(w_dn, i * 1024, 8, 896, 192))], i)

        def ada_two(p, a):
            for i in (0, 1):
                if a < 4:
                    src = ada_w[0, 1][(a + i) * 512:(a + i + 1) * 512, bass.ds(p * 512, 512)]
                else:
                    layer, col = p // (PAIRS // 2), 2 * D + (p % (PAIRS // 2)) * 512
                    src = ada_w[0][bass.ds(layer, 1), (a + i - 4) * 512:(a + i - 3) * 512, bass.ds(col, 512)]
                    src = src.rearrange("s r n -> (s r) n")
                if isinstance(p, int) and p == 0 and a + i == 1:
                    sp.wait_ge(kv_lo, 4)
                ada_unit(32 + 8 * p + a + i, i, [src.rearrange("(k p) n -> p k n", p=P)])

        def pair_units(p, before=None):
            u = u_pair(p)
            first = isinstance(p, int) and p == 0
            q_src = w_q[:, bass.ds(p * (2 * QD), 2 * QD)].rearrange("(k p) n -> p k n", p=P)
            kv_col = 0 if first else (before * 2 + 2) * KVD
            kv_src = w_kv[:, bass.ds(kv_col, 2 * KVD)].rearrange("(k p) n -> p k n", p=P)
            q_dst = raw_of(0, 4, 2 * QD)
            parts = []
            for d in (0, 1):
                parts.append((q_dst[:, :, P * (1 + d):P * (2 + d)], q_src[:, :, QD * d:QD * d + NOPE]))
                for h in (0, 1):
                    o, i = HALF * (2 * h + d), QD * d + NOPE + HALF * h
                    parts.append((q_dst[:, :, o:o + HALF], q_src[:, :, i:i + HALF]))
            with nc.allow_non_contiguous_dma(reason="the rotary columns are runs of 128 bytes"):
                unit(u, parts, 0, q_full)
            if not first:
                ada_two(before, 6)
            unit(u + 1, [(raw_of(1, 4, 2 * KVD), kv_src)], 1)
            ada_two(p, 0)
            if not first:
                o_rows = w_out[bass.ds(before * 256, 256), :].rearrange("(k p) n -> p k n", p=P)
                unit(u + 2, [(raw_of(0, 2, 1024), o_rows[:, :, 0:1024])], 0)
            ada_two(p, 2)
            if not first:
                unit(u + 3, [(raw_of(1, 2, 1024), o_rows[:, :, 1024:2048])], 1)
            ada_two(p, 4)

        pair_units(0)
        with sp.Fori(0, PAIRS - 1) as before:
            pair_units(before + 1, before)
        last = rows(w_out, (PAIRS - 1) * 256, 2, 0, D)
        cuts = [(k, a, b) for k in (0, 1) for a, b in ((0, 512), (512, 768), (768, 1024))]
        unit(U_MLP - 2, [(raw_of(0, 2, 1024)[:, k, a:b], last[:, k, a:b]) for k, a, b in cuts], 0, q_full)
        ada_two(PAIRS - 1, 6)
        unit(U_MLP - 1, [(raw_of(1, 2, 1024), last[:, :, 1024:])], 1)

        def row(i):
            sp.dma_start(row_at[i], row_dram[i:i + 1, :].broadcast_to([P, D])).then_inc(row_full[i], 16)

        def up_unit(c, kk):
            src = up[kk * 512:(kk + 1) * 512, bass.ds(c * CH, CH)]
            unit(U_MLP + 8 * c + kk, [(raw_of(kk, 4, 512), src.rearrange("(k p) n -> p k n", p=P))], kk % 2)

        def down_unit(c, n):
            src = dn[bass.ds(c * CH, CH), n * 512:(n + 1) * 512]
            unit(U_MLP + 8 * c + 4 + n, [(raw_of(n, 4, 512), src.rearrange("(k p) n -> p k n", p=P))], n % 2)

        up_unit(0, 0)
        sp.wait_ge(four_out, 1)
        sp.dma_start(row_dram.rearrange("s (k e) -> (s k) e", e=P), acc[0:4 * KT, 0, 0:P]).then_inc(four_put, 16)
        sp.dma_start(res_tile(0), x2[0:P, :]).then_inc(res_full[0], 16)
        sp.wait_ge(four_put, 16)
        row(0)
        sp.wait_ge(t_ps, 2 * PAIRS)
        sp.dma_start(res_tile(1), x2[P:2 * P, :]).then_inc(res_full[1], 16)
        row(1)
        for t in range(TT):
            sp.wait_ge(res_added[t], 1)
            sp.dma_start(x1_dram[t * P:(t + 1) * P, :], y[:, t, :]).then_inc(x1_put[t], 16)
            if t + 2 < TT:
                sp.dma_start(res_tile(t), x2[(t + 2) * P:(t + 3) * P, :]).then_inc(res_full[t % 2], 16)
            if t == 1:
                up_unit(0, 1)
        row(3)

        for kk in (2, 3):
            up_unit(0, kk)
        for n in range(4):
            down_unit(0, n)
        with sp.Fori(1, CHUNKS) as c_:
            for kk in range(4):
                up_unit(c_, kk)
            for n in range(4):
                down_unit(c_, n)
        sp.wait_ge(up_ps, 4 * CHUNKS)
        for t in range(TT):
            sp.wait_ge(x1_put[t], 16)
            sp.dma_start(x1_again(t), x1_dram[t * P:(t + 1) * P, :]).then_inc(x1_full[t], 16)
        for t in range(TT):
            for i, (a, b) in enumerate(((0, D - CH), (D - CH, D))):
                sp.wait_ge(out_done, 2 * t + i + 1)
                sp.dma_start(out2[t * P:(t + 1) * P, a:b], y[:, t, a:b]).then_inc(out_put, 16)
        sp.wait_ge(out_put, 16 * 2 * TT)

    @block.gpsimd
    def _(pool):
        G = nc.gpsimd
        nc.gpsimd.memset(ident[:], 0.0).then_inc(consts, 1)
        nc.gpsimd.memset(mask_u[:].bitcast(F32), 0.0).then_inc(consts, 1)
        nc.gpsimd.memset(mask_v[:].bitcast(F32), 0.0).then_inc(consts, 1)
        nc.gpsimd.memset(krope[:].bitcast(F32), 0.0).then_inc(consts, 1)
        pool.wait_ge(consts, 4)
        nc.gpsimd.affine_select(out=ident[:], in_=ident[:], compare_op=ALU.not_equal, fill=1.0, base=0,
                                pattern=[[-1, P]], channel_multiplier=1).then_inc(consts, 1)
        nc.gpsimd.memset(mask_u[0:1, 0:64].bitcast(F32), 1.0).then_inc(consts, 1)
        nc.gpsimd.memset(mask_v[0:1, 64:128].bitcast(F32), MASKED).then_inc(consts, 1)

        def lo(u, slot, words=UNIT):
            pool.wait_ge(hi_done, u + 1)
            nc.gpsimd.tensor_tensor(split[:, slot, 1, :words], raw[:, slot, :words],
                                    split[:, slot, 0, :words].bitcast(F32), ALU.subtract).then_inc(lo_done, 1)

        def lo_parts(u, parts):
            pool.wait_ge(hi_done, u + 1)
            for r, s in parts:
                op = nc.gpsimd.tensor_tensor(s[1], r, s[0].bitcast(F32), ALU.subtract)
            op.then_inc(lo_done, 1)

        def feature_lo(a, b):
            for k in range(a, b):
                pool.wait_ge(h_hi, k + 1)
                G.tensor_tensor(big[:, 16 + k, :].rearrange("p (t c) -> p t c", t=TT), xt_view[:, k],
                                big[:, k, :].bitcast(F32).rearrange("p (t c) -> p t c", t=TT),
                                ALU.subtract).then_inc(h_lo, 1)

        for kk in range(4):
            lo(U_A[kk], 0)
            if kk == 3:
                feature_lo(12, 14)
            lo(U_B[kk], 1, 4 * 384)
            feature_lo(14 if kk == 3 else 4 * kk, 4 * kk + 4)
        for u in (8, 9):
            lo_parts(u, c_parts(u % 2))
        lo(10, 0)
        for n in range(4):
            pool.wait_ge(lat_hi, n + 1)
            G.tensor_tensor(lat[:, 1, n, :], lat_square(n), lat[:, 0, n, :].bitcast(F32),
                            ALU.subtract).then_inc(lat_lo, 1)
        lo(11, 1)
        pool.wait_ge(lat_lo, 4)
        pool.wait_ge(kv_lo, 4)
        pool.wait_ge(kr_lo, 1)
        for t in range(TT):
            G.memset(y[:, t, :], 0.0).then_inc(y_zero, 1)
        with pool.Fori(1, PAIRS) as p:
            for j in range(4):
                lo(u_pair(p) + j, j % 2)
        for j in (0, 1):
            lo(U_MLP - 2 + j, j)
        for t in (0, 1, 2):
            pool.wait_ge(res_mul, t + 1)
            pool.wait_ge(res_full[t % 2], 16 * (t // 2 + 1))
            G.tensor_tensor(y[:, t, :], y[:, t, :], res_tile(t), ALU.add).then_inc(res_added[t], 1)
        lo(U_MLP, 0)
        lo(U_MLP + 1, 1)
        for t in range(TT):
            pool.wait_ge(xt_ps, KT + 4 * (t + 1))
            G.memset(y[:, t, :], 0.0).then_inc(y_zero, 1)
        for j in range(2, 8):
            lo(U_MLP + j, j % 2)
        with pool.Fori(1, CHUNKS) as c_:
            for j in range(8):
                lo(U_MLP + 8 * c_ + j, j % 2)
        pool.wait_ge(row_full[3], 16)
        for t in range(TT):
            pool.wait_ge(dn_added, 16 * (CHUNKS - 1) + 12 + t + 1)
            G.tensor_tensor(scr[:, t * 512:(t + 1) * 512], y[:, t, D - 512:D], row_at[3][:, D - 512:D],
                            ALU.mult).then_inc(last_gate, 1)


    @block.scalar
    def _(act):
        def unit_hi(u, slot, used=None, count=None, parts=None, full=None, words=UNIT):
            act.wait_ge(*(full or (raw_full[slot], raw_count(u, slot))))
            if used is not None:
                act.wait_ge(used, count)
            for r, s in parts or [(raw[:, slot, :words], [split[:, slot, 0, :words]])]:
                op = nc.scalar.activation(s[0], r, ACT.Copy)
            op.then_inc(hi_done, 1)

        act.wait_ge(par_cols, 1)
        nc.scalar.activation(csil[:, 1, :], pcol[:, C_C:C_C + KT], ACT.Exp, scale=-1.0).then_inc(c_exp, 1)

        def row_root(stage, t):
            total, root, _ = stat_cols(stage, t)
            q = STATS.index((stage, t))
            squares = krope[:].rearrange("p a b n -> p (a b n)")
            nc.scalar.activation(squares, y[:, t, :], ACT.Square, accum_out=total).then_inc(ss_done, 1)
            act.wait_ge(ss_done, TT + q + 1)
            nc.scalar.activation(root, total, ACT.Sqrt, bias=eps_col, scale=1.0 / D).then_inc(sd_done, 1)

        for t in range(TT):
            act.wait_ge(x_full[t], 16)
            squares = big[:, 4 * t:4 * t + 4, :].rearrange("p s n -> p (s n)")
            nc.scalar.activation(squares, y[:, t, :], ACT.Square, accum_out=stat[:, 4 + t:5 + t]).then_inc(ss_done, 1)
        act.wait_ge(var_done, 1)
        nc.scalar.activation(stat[:, 12:16], stat[:, 8:12], ACT.Sqrt).then_inc(sd_done, 1)
        for k in range(KT):
            act.wait_ge(xt_ps, k + 1)
            nc.scalar.activation(xt_view[:, k], ps[:, k % 4, :].rearrange("p (t c) -> p t c", t=TT),
                                 ACT.Copy).then_inc(xt_out, 1)

        act.wait_ge(ang_done, 1)
        for i in (0, 1):
            nc.scalar.activation(trig[:, i, :], trig[:, i, :], ACT.Sin).then_inc(trig_done, 1)

        def feature_hi(a, b):
            for k in range(a, b):
                act.wait_ge(mod_done, k + 1)
                nc.scalar.activation(big[:, k, :].rearrange("p (t c) -> p t c", t=TT), xt_view[:, k],
                                     ACT.Copy).then_inc(h_hi, 1)

        for kk in range(4):
            for u in (U_A[kk], U_B[kk]):
                words = 4 * 512 if u % 2 == 0 else 4 * 384
                if u < 2:
                    unit_hi(u, u % 2, words=words)
                else:
                    unit_hi(u, u % 2, unit_used, u - 1, words=words)
                if kk == 3 and u == U_A[3]:
                    feature_hi(12, 14)
            feature_hi(14 if kk == 3 else 4 * kk, 4 * kk + 4)

        def latent_out(n, b):
            act.wait_ge(down_ps, n + 1)
            nc.scalar.activation(lat_tile(n), ps[:, b, :], ACT.Copy)
            nc.scalar.activation(lat_square(n), ps[:, b, :], ACT.Square).then_inc(lat_out, 1)

        def latent_root(i):
            act.wait_ge(lat_var, i + 1)
            nc.scalar.activation(lat_row(i, 0), lat_row(i, 0), ACT.Sqrt).then_inc(lat_sd, 1)

        def latent_hi(i):
            for n in range(4 * i, 4 * i + 4):
                act.wait_ge(lat_mul, n + 1)
                nc.scalar.activation(lat[:, 0, n, :], lat_square(n), ACT.Copy).then_inc(lat_hi, 1)

        for n in range(3):
            latent_out(n, n)
        unit_hi(U_C[0], 0, down_ps, 4, c_parts(0))
        for n in range(3, 7):
            latent_out(n, n)
        unit_hi(U_C[1], 1, down_ps, 7, c_parts(1))
        latent_root(0)
        unit_hi(10, 0, unit_used, 7, full=(q_full, 16 * Q_PARTS))
        latent_hi(0)
        latent_out(7, 0)
        latent_root(1)
        act.wait_ge(kr_rot, 1)
        for par in (0, 1):
            for half in (0, 1):
                r0 = 64 * half + 32 * par
                op = nc.scalar.activation(krope[r0:r0 + 32, par, 0, :], lat_row(0, 0)[r0:r0 + 32], ACT.Copy)
        op.then_inc(kr_hi, 1)
        unit_hi(11, 1, kr_ps, 1)
        latent_hi(1)

        def pair(p):
            first = isinstance(p, int) and p == 0
            u = u_pair(p)

            def proj_hi(k, dst, src):
                act.wait_ge(pj_ps, 7 * p + k + 1)
                nc.scalar.activation(dst, src, ACT.Copy).then_inc(pj_hi, 1)

            for k in (1, 2, 0) if first else (0, 1, 2):
                if k == 0:
                    act.wait_ge(q_rot, p + 1)
                    proj_hi(0, big[:, S_QR[0], :], scr[:, ROPE_A:ROPE_A + 512])
                else:
                    proj_hi(k, big[:, S_QN[0] + k - 1, :], ps[:, k - 1, :])
            proj_hi(3, big[:, S_KN[0], :], ps[:, 0, :])
            proj_hi(4, big[:, S_KN[0] + 1, :], ps[:, 1, :])
            if not first:
                unit_hi(u + 2, 0, pj_ps, 7 * p + 3, full=(raw_full[0], 16 * (5 + p)))

            def exps(hd):
                n = 2 * p + hd
                act.wait_ge(nbias, n + 1)
                if not (first and hd == 0):
                    act.wait_ge(t_ps, n)
                for i in range(TT):
                    b, o = S_AT[i]
                    ln = (i + 1) * P
                    op = nc.scalar.activation(scr[:, P_AT[i]:P_AT[i] + ln], ps[:, b, o:o + ln], ACT.Exp,
                                              bias=stat[:, 12 + i:13 + i], scale=SCALE,
                                              accum_out=stat[:, 16 + i:17 + i])
                op.then_inc(s_exp, 1)

            def turned_hi(hd):
                n = 2 * p + hd
                act.wait_ge(t_ps, n + 1)
                if not (first and hd == 0):
                    act.wait_ge(pv_ps, n)
                for i in T_ORDER:
                    dst = big[:, S_PT[0]:S_PT[0] + i + 1, i * P:(i + 1) * P]
                    b, o = t_at(i, hd)
                    src = ps[:, b, o:o + (i + 1) * P].rearrange("p (j c) -> p j c", c=P)
                    nc.scalar.activation(dst, src, ACT.Copy).then_inc(t_hi, 1)

            exps(0)
            proj_hi(5, v_view(0)[:, 0:2], ps[:, 5, :].rearrange("p (t n) -> p t n", t=2))
            proj_hi(6, v_view(0)[:, 2:4], ps[:, 6, :].rearrange("p (t n) -> p t n", t=2))
            if not first:
                unit_hi(u + 3, 1, pj_ps, 7 * p + 7)
            turned_hi(0)
            exps(1)
            if first:
                unit_hi(12, 0, pj_ps, 3, full=(q_full, 16 * Q_PARTS * 2))
            else:
                unit_hi(u + 4, 0, wo_ps, 16 * (p - 1) + 8, full=(q_full, 16 * Q_PARTS * (p + 2)))
            turned_hi(1)
            act.wait_ge(pv_ps, 2 * p + 2)
            for hd in (0, 1):
                nc.scalar.activation(big[:, S_AO[0] + hd, :], ps[:, (7, 4)[hd], :], ACT.Copy).then_inc(ao_hi, 1)
            if first:
                unit_hi(13, 1, pj_ps, 7)
            else:
                unit_hi(u + 5, 1, wo_ps, 16 * p)

        pair(0)
        with act.Fori(1, PAIRS) as p:
            pair(p)

        def turned_h(t):
            for g in range(4):
                act.wait_ge(xt_ps, KT + 4 * t + g + 1)
                for j in range(4):
                    k = 4 * g + j
                    op = nc.scalar.activation(big[:, k, t * P:(t + 1) * P], ps[:, turn_bank(t) + g, j * P:(j + 1) * P],
                                              ACT.Identity, bias=four[:, 2, k:k + 1])
                op.then_inc(h_hi, 1)

        for stage, t in STATS[:8]:
            if stage == 1:
                act.wait_ge(wo_added, 16 * (PAIRS - 1) + LAST_WO.index((t, 3)) + 1)
            else:
                act.wait_ge(res_added[t], 1)
            row_root(stage, t)
            if (stage, t) == (2, 1):
                unit_hi(U_MLP, 0, wo_ps, 16 * PAIRS)
                turned_h(0)
            if (stage, t) == (2, 2):
                turned_h(1)
        unit_hi(U_MLP + 1, 1, wo_ps, 16 * PAIRS)
        turned_h(2)
        turned_h(3)

        def block_square(n, t):
            m = 4 * n + t
            act.wait_ge(dn_added, 16 * (CHUNKS - 1) + m + 1)
            if m >= 4:
                act.wait_ge(blk_sq, m - 3)
            nc.scalar.activation(krope[:, t // 2, t % 2, :], y[:, t, n * 512:(n + 1) * 512], ACT.Square,
                                 accum_out=stat[:, 80 + 4 * t + n:81 + 4 * t + n]).then_inc(blk_sq, 1)

        def mlp(c_, last=False):
            u = U_MLP + 8 * c_
            for j in range(2, 5):
                unit_hi(u + j, j % 2, unit_used, 7 + 3 * c_ + j - 1)
            for j in range(4):
                n = 4 * c_ + j
                act.wait_ge(up_ps, n + 1)
                if not (isinstance(c_, int) and j < 2):
                    act.wait_ge(act_sq, n - 1)
                nc.scalar.activation(scr[:, (j % 2) * 512:(j % 2 + 1) * 512], ps[:, j, :],
                                     ACT.Relu).then_inc(act_relu, 1)
                act.wait_ge(act_relu, n + 1)
                nc.scalar.activation(lat[:, 0, j, :], scr[:, (j % 2) * 512:(j % 2 + 1) * 512],
                                     ACT.Square).then_inc(hid_hi, 1)
            unit_hi(u + 5, 1, up_ps, 4 * c_ + 4)
            for n in range(4):
                if n in (1, 2):
                    unit_hi(u + 5 + n, (5 + n) % 2, dn_ps, 16 * c_ + 4 * n)
                for t in range(TT) if last else ():
                    block_square(n, t)
                    if n == 3:
                        total, root, _ = stat_cols(3, t)
                        act.wait_ge(ss_done, TT + 8 + t + 1)
                        nc.scalar.activation(root, total, ACT.Sqrt, bias=eps_col, scale=1.0 / D).then_inc(sd_done, 1)

        mlp(0)
        def next_up(c_):
            for j in (0, 1):
                unit_hi(U_MLP + 8 * c_ + j, j, dn_ps, 16 * (c_ - 1) + 12 + 4 * j)

        with act.Fori(1, CHUNKS - 1) as c_:
            next_up(c_)
            mlp(c_)
        next_up(CHUNKS - 1)
        mlp(CHUNKS - 1, True)

    @block.vector
    def _(dve):
        own = [0]

        def link(op):
            own[0] += 1
            op.then_inc(dve_own, 1)
            dve.wait_ge(dve_own, own[0])

        V = nc.vector
        V.memset(eps_col, EPS)
        V.memset(ones[:], 1.0).then_inc(ones_done, 1)
        dve.wait_ge(par_ps, 1)
        V.tensor_copy(pcol[:], ps[:, 7, 0:N_PC]).then_inc(par_cols, 1)
        dve.wait_ge(c_exp, 1)
        link(V.tensor_scalar(csil[:, 1, :], csil[:, 1, :], 1.0, None, ALU.add))
        link(V.reciprocal(csil[:, 0, :], csil[:, 1, :]))
        link(V.tensor_tensor(csil[:, 0, :], pcol[:, C_C:C_C + KT], csil[:, 0, :], ALU.mult))

        turn, magic, edge = 6.283185307179586, 12582912.0, 3.1415925
        c1, c2 = 6.28125, 0.0019350051879882812
        ang, cnt, part = scr[:, 1024:1536], scr[:, 1536:2048], scr[:, 2048:2560]
        dve.wait_ge(par_full, 16 * 8)
        link(V.tensor_copy(ang, scr[:, 512:1024].bitcast(I32)))
        link(V.tensor_scalar(ang, ang, stat[:, 0:1], None, ALU.mult))
        for i, shift in ((0, 0.25), (1, 0.0)):
            to = trig[:, i, :]
            link(V.tensor_scalar(cnt, ang, 1.0 / turn, shift, ALU.mult, ALU.add))
            link(V.tensor_scalar(cnt, cnt, magic, None, ALU.add))
            link(V.tensor_scalar(cnt, cnt, -magic, None, ALU.add))
            for n, c in enumerate((c1, c2, turn - c1 - c2)):
                link(V.tensor_scalar(part, cnt, -c, None, ALU.mult))
                link(V.tensor_tensor(to, to if n else ang, part, ALU.add))
            link(V.tensor_scalar(to, to, shift * turn, None, ALU.add))
            link(V.tensor_scalar(to, to, edge, -edge, ALU.min, ALU.max))
        V.tensor_scalar(trig[0:64, 1, :], trig[0:64, 1, :], -1.0, None, ALU.mult).then_inc(ang_done, 1)

        dve.wait_ge(ss_done, TT)
        V.tensor_scalar(stat[:, 8:12], stat[:, 4:8], 1.0 / D, EPS, ALU.mult, ALU.add).then_inc(var_done, 1)
        dve.wait_ge(sd_done, 1)
        link(V.reciprocal(stat[:, 16:20], stat[:, 12:16]))
        for t in range(TT):
            V.tensor_scalar(y[:, t, :], y[:, t, :], stat[:, 16 + t:17 + t], None, ALU.mult).then_inc(xn_done, 1)

        def ada_steps(chunk0, s0, s1):
            for s in range(s0, s1):
                k, row, which = s % 4, s % 16, s // 16
                if isinstance(chunk0, int) and chunk0 < 8:
                    m = 4 * chunk0 + s // 4
                    slot, full = m % 3, m // 3 + 1 + (0 if m < 24 else (m - 24) // 3 + 1)
                else:
                    slot, full = (s // 4) % 2, 2 * chunk0 - 16 + 14 + s // 8 + 1
                cols = ada_slot(slot)[:, k * 512:(k + 1) * 512]
                if k == 0:
                    dve.wait_ge(ada_full[slot], 16 * full)
                if row == 0:
                    if not (isinstance(chunk0, int) and chunk0 == 0):
                        dve.wait_ge(col_ps, chunk0 + which - 1)
                    op = V.tensor_scalar(acc[:, which, :], cols, csil[:, 0, 0:1], None, ALU.mult)
                else:
                    dve.wait_ge(ada_step, 16 * chunk0 + s)
                    op = V.scalar_tensor_tensor(out=acc[:, which, :], in0=cols, scalar=csil[:, 0, row:row + 1],
                                                in1=acc[:, which, :], op0=ALU.mult, op1=ALU.add)
                op.then_inc(ada_step, 1)

        def modulated(k0, n, chunks, saved):
            cols = slice(k0, k0 + n)
            dve.wait_ge(col_ps, chunks)
            V.tensor_tensor(mod[:, 0, cols], ps[:, 7, 0:n], pcol[:, C_B + k0:C_B + k0 + n], ALU.add)
            link(V.tensor_tensor(mod[:, 1, cols], ps[:, 7, n:2 * n], pcol[:, C_B + KT + k0:C_B + KT + k0 + n], ALU.add))
            V.scalar_tensor_tensor(out=mod[:, 1, cols], in0=mod[:, 1, cols], scalar=1.0,
                                   in1=pcol[:, C_PRE + k0:C_PRE + k0 + n], op0=ALU.add,
                                   op1=ALU.mult).then_inc(col_saved, saved)
            dve.wait_ge(col_saved, chunks)
            for k in range(k0, k0 + n):
                dve.wait_ge(xt_out, k + 1)
                V.tensor_scalar(xt_view[:, k], xt_view[:, k], mod[:, 1, k:k + 1], mod[:, 0, k:k + 1],
                                ALU.mult, ALU.add).then_inc(mod_done, 1)

        for kk in range(3):
            ada_steps(2 * kk, 0, 32)
            modulated(4 * kk, 4, 2 * kk + 2, 2)
        for g in (0, 1):
            ada_steps(6, 16 * g, 16 * g + 16)
            modulated(12 + 2 * g, 2, 7 + g, 1)

        def latent_square_sum(i):
            first = lat_square(4 * i)
            for n in range(4 * i + 1, 4 * i + 4):
                dve.wait_ge(lat_out, n + 1)
                op = V.tensor_tensor(first, first, lat_square(n), ALU.add)
                if n == 4 * i + 3:
                    op.then_inc(sq_sum, 1)
                else:
                    link(op)

        def latent(i, gcol):
            dve.wait_ge(lat_sum, i + 1)
            V.tensor_scalar(lat_row(i, 0), ps[:, 7, :], 1.0 / LORA, EPS, ALU.mult, ALU.add).then_inc(lat_var, 1)
            dve.wait_ge(lat_sd, i + 1)
            link(V.reciprocal(lat_row(i, 1), lat_row(i, 0)))
            for n in range(4 * i, 4 * i + 4):
                g = gcol + n - 4 * i
                V.scalar_tensor_tensor(out=lat_square(n), in0=lat_tile(n), scalar=pcol[:, g:g + 1],
                                       in1=lat_row(i, 1), op0=ALU.mult, op1=ALU.mult).then_inc(lat_mul, 1)

        def rotate(b, A=scr[:, ROPE_A:ROPE_A + 512], B=scr[:, ROPE_B:ROPE_B + 512]):
            V.tensor_tensor(A, ps[:, b, :], trig[:, 0, :], ALU.mult)
            V.tensor_tensor(B[0:64], ps[64:128, b, :], trig[0:64, 1, :], ALU.mult)
            return V.tensor_tensor(B[64:128], ps[0:64, b, :], trig[64:128, 1, :], ALU.mult)

        latent_square_sum(0)
        latent(0, C_QN)
        latent_square_sum(1)
        dve.wait_ge(kr_ps, 1)
        dve.wait_ge(trig_done, 2)
        key = lat_row(0, 0)
        link(rotate(3, key, lat_row(0, 1)))
        V.tensor_tensor(key, key, lat_row(0, 1), ALU.add).then_inc(kr_rot, 1)
        latent(1, C_KVN)
        for n in range(4, 8):
            dve.wait_ge(lat_hi, n + 1)
            V.tensor_tensor(lat[:, 1, n, :], lat_square(n), lat[:, 0, n, :].bitcast(F32),
                            ALU.subtract).then_inc(kv_lo, 1)

        def key_lo():
            dve.wait_ge(kr_hi, 1)
            for par in (0, 1):
                for half in (0, 1):
                    r0 = 64 * half + 32 * par
                    op = V.tensor_tensor(krope[r0:r0 + 32, par, 1, :], key[r0:r0 + 32],
                                         krope[r0:r0 + 32, par, 0, :].bitcast(F32), ALU.subtract)
            op.then_inc(kr_lo, 1)

        own_base = own[0]

        def gate_sums(col, count):
            dve.wait_ge(col_ps, count)
            V.tensor_copy(sums[:, 1, bass.ds(col, 4)], ps[:, 5, 0:4]).then_inc(col_saved, 1)

        def pair(p):
            first = isinstance(p, int) and p == 0
            m0 = 8 + 2 * p

            def mine(op, k):
                op.then_inc(dve_own, 1)
                dve.wait_ge(dve_own, own_base + 5 * p + k)

            def proj_lo(k, dst, src, hi, number=None):
                dve.wait_ge(pj_hi, 7 * p + (k if number is None else number) + 1)
                V.tensor_tensor(dst, src, hi.bitcast(F32), ALU.subtract).then_inc(pj_lo, 1)

            at = [0]

            def more(n):
                ada_steps(m0, at[0], at[0] + n)
                at[0] += n

            if first:
                proj_lo(1, big[:, S_QN[1], :], ps[:, 0, :], big[:, S_QN[0], :], 0)
                proj_lo(2, big[:, S_QN[1] + 1, :], ps[:, 1, :], big[:, S_QN[0] + 1, :], 1)
            dve.wait_ge(pj_ps, 7 * p + 1)
            mine(rotate(2), 1)
            V.tensor_tensor(scr[:, ROPE_A:ROPE_A + 512], scr[:, ROPE_A:ROPE_A + 512],
                            scr[:, ROPE_B:ROPE_B + 512], ALU.add).then_inc(q_rot, 1)
            if not first:
                more(1)
            proj_lo(0, big[:, S_QR[1], :], scr[:, ROPE_A:ROPE_A + 512], big[:, S_QR[0], :], 2 if first else 0)
            if first:
                key_lo()
            else:
                proj_lo(1, big[:, S_QN[1], :], ps[:, 0, :], big[:, S_QN[0], :])
                gate_sums(4 * p - 4, 8 + 2 * p)
                more(3)
                proj_lo(2, big[:, S_QN[1] + 1, :], ps[:, 1, :], big[:, S_QN[0] + 1, :])
            proj_lo(3, big[:, S_KN[1], :], ps[:, 0, :], big[:, S_KN[0], :])
            if not first:
                more(3)
            proj_lo(4, big[:, S_KN[1] + 1, :], ps[:, 1, :], big[:, S_KN[0] + 1, :])

            def maxima(hd):
                dve.wait_ge(s_ps, 2 * p + hd + 1)
                for i in range(TT):
                    b, o = S_AT[i]
                    op = V.reduce_max(stat[:, 8 + i:9 + i], ps[:, b, o:o + (i + 1) * P], AX_X)
                mine(op, 2 + 2 * hd)
                V.tensor_scalar(stat[:, 12:16], stat[:, 8:12], -SCALE, None, ALU.mult).then_inc(nbias, 1)

            def normed(hd):
                dve.wait_ge(s_exp, 2 * p + hd + 1)
                mine(V.reciprocal(stat[:, 20:24], stat[:, 16:20]), 3 + 2 * hd)
                for i in range(TT):
                    pr = scr[:, P_AT[i]:P_AT[i] + (i + 1) * P]
                    op = V.tensor_scalar(pr, pr, stat[:, 20 + i:21 + i], None, ALU.mult)
                op.then_inc(p_norm, 1)

            def turned_lo(hd):
                for n, i in enumerate(T_ORDER):
                    dve.wait_ge(t_hi, 8 * p + 4 * hd + max(n + 1, 2))
                    dst, hi = (big[:, s:s + i + 1, i * P:(i + 1) * P] for s in (S_PT[1], S_PT[0]))
                    b, o = t_at(i, hd)
                    src = ps[:, b, o:o + (i + 1) * P].rearrange("p (j c) -> p j c", c=P)
                    op = V.tensor_tensor(dst, src, hi.bitcast(F32), ALU.subtract)
                op.then_inc(t_lo, 1)

            def drains(n, steps):
                for t in range(TT):
                    if not first:
                        wo_add(p - 1, 4 * n + t)
                    if t < steps:
                        more(1)

            more(4 if first else 3)
            maxima(0)
            more(4 if first else 2)
            normed(0)
            for k, s in ((5, 0), (6, 2)):
                proj_lo(k, v_view(1)[:, s:s + 2], ps[:, k, :].rearrange("p (t n) -> p t n", t=2),
                        v_view(0)[:, s:s + 2])
            if first:
                more(2)
            drains(0, 4)
            turned_lo(0)
            more(2)
            maxima(1)
            drains(1, 4 if first else 3)
            normed(1)
            dve.wait_ge(col_ps, 8 + 2 * p + 1)
            V.tensor_copy(sums[:, 0, bass.ds(4 * p, 4)], ps[:, 5, 0:4]).then_inc(col_saved, 1)
            if not first:
                more(1)
            drains(2, 4)
            turned_lo(1)
            drains(3, 4 if first else 2)
            more(2)
            for hd in (0, 1):
                dve.wait_ge(ao_hi, 2 * p + hd + 1)
                V.tensor_tensor(big[:, S_AO[1] + hd, :], ps[:, (7, 4)[hd], :], big[:, S_AO[0] + hd, :].bitcast(F32),
                                ALU.subtract).then_inc(ao_lo, 1)
            more(32 - at[0])

        def wo_add(q, m, order=None):
            n, t = divmod(m, TT)
            b = m % 2 if order is None else order % 4
            order = m if order is None else order
            dst = y[:, t, n * 512:(n + 1) * 512]
            dve.wait_ge(wo_ps, 16 * q + order + 1)
            V.tensor_tensor(dst, dst, ps[:, b, :], ALU.add).then_inc(wo_added, 1)

        pair(0)
        dve.wait_ge(y_zero, TT)
        with dve.Fori(1, PAIRS) as p:
            pair(p)
        own[0] += 5 * PAIRS

        def wo_adds(a, b):
            for order in range(a, b):
                t, n = LAST_WO[order]
                wo_add(PAIRS - 1, 4 * n + t, order)

        wo_adds(0, 2)
        gate_sums(4 * PAIRS - 4, 8 + 2 * PAIRS)
        dve.wait_ge(col_saved, 8 + 2 * PAIRS)
        link(V.tensor_tensor(four[:, 2, :], sums[:, 0, 0:KT], pcol[:, C_B + 48:C_B + 48 + KT], ALU.add))
        link(V.tensor_tensor(four[:, 1, :], sums[:, 0, KT:], pcol[:, C_B + 64:C_B + 64 + KT], ALU.add))
        link(V.scalar_tensor_tensor(out=four[:, 1, :], in0=four[:, 1, :], scalar=1.0,
                                    in1=pcol[:, C_PRE + KT:C_PRE + 2 * KT], op0=ALU.add, op1=ALU.mult))
        for s in (0, 1):
            b0 = C_B + 48 * s + 32
            link(V.tensor_tensor(four[:, 3 * s, :], sums[:, 1, s * KT:(s + 1) * KT], pcol[:, b0:b0 + KT], ALU.add))
            op = V.tensor_tensor(four[:, 3 * s, :], four[:, 3 * s, :],
                                 pcol[:, C_POST + s * KT:C_POST + (s + 1) * KT], ALU.mult)
        op.then_inc(four_done, 1)

        wo_adds(2, 4)
        dve.wait_ge(four_ps, 1)
        V.tensor_copy(acc[0:4 * KT, 0, 0:P], ps[0:4 * KT, 5, 0:P]).then_inc(four_out, 1)

        def rstd(stage, t):
            _, root, one = stat_cols(stage, t)
            dve.wait_ge(sd_done, 2 + STATS.index((stage, t)))
            link(V.reciprocal(one, root))
            return one

        def residual(t):
            one = rstd(1, t)
            dve.wait_ge(row_full[0], 16)
            V.scalar_tensor_tensor(out=y[:, t, :], in0=y[:, t, :], scalar=one, in1=row_at[0],
                                   op0=ALU.mult, op1=ALU.mult).then_inc(res_mul, 1)
            if t == 3:
                dve.wait_ge(res_mul, t + 1)
                dve.wait_ge(res_full[t % 2], 16 * (t // 2 + 1))
                V.tensor_tensor(y[:, t, :], y[:, t, :], res_tile(t), ALU.add).then_inc(res_added[t], 1)

        def gained(t):
            one = rstd(2, t)
            dve.wait_ge(row_full[1], 16)
            dve.wait_ge(x1_put[t], 16)
            V.scalar_tensor_tensor(out=y[:, t, :], in0=y[:, t, :], scalar=one, in1=row_at[1],
                                   op0=ALU.mult, op1=ALU.mult).then_inc(h_mul, 1)

        def turned_lo(t):
            for g in range(4):
                dve.wait_ge(h_hi, KT + 4 * t + g + 1)
                for j in range(4):
                    k = 4 * g + j
                    op = V.scalar_tensor_tensor(out=big[:, 16 + k, t * P:(t + 1) * P],
                                                in0=ps[:, turn_bank(t) + g, j * P:(j + 1) * P],
                                                scalar=four[:, 2, k:k + 1],
                                                in1=big[:, k, t * P:(t + 1) * P].bitcast(F32),
                                                op0=ALU.add, op1=ALU.subtract)
                op.then_inc(h_lo, 1)

        wo_adds(4, 8)
        residual(0)
        wo_adds(8, 12)
        residual(1)
        wo_adds(12, 16)
        gained(0)
        residual(2)
        gained(1)
        turned_lo(0)
        residual(3)
        gained(2)
        turned_lo(1)
        gained(3)
        turned_lo(2)
        turned_lo(3)
        dve.wait_ge(y_zero, 2 * TT)

        def block(m):
            n, t = divmod(m, TT)
            return y[:, t, n * 512:(n + 1) * 512]

        def gated(m):
            n = m // TT
            dve.wait_ge(blk_sq, m + 1)
            V.tensor_tensor(block(m), block(m), row_at[3][:, n * 512:(n + 1) * 512], ALU.mult).then_inc(blk_gate, 1)

        def out_tile(t, part):
            total, _, one = stat_cols(3, t)
            if part == 0:
                dve.wait_ge(blk_sq, 12 + t + 1)
                V.reduce_sum(total, stat[:, 80 + 4 * t:84 + 4 * t], AX_X).then_inc(ss_done, 1)
                rstd(3, t)
                dve.wait_ge(x1_full[t], 16)
                dve.wait_ge(blk_gate, 12)
                z, a, b = y[:, t, 0:D - 512], 0, D - 512
            else:
                dve.wait_ge(last_gate, t + 1)
                z, a, b = scr[:, t * 512:(t + 1) * 512], D - 512, D
            V.scalar_tensor_tensor(out=y[:, t, a:b], in0=z, scalar=one, in1=x1_again(t)[:, a:b],
                                   op0=ALU.mult, op1=ALU.add).then_inc(out_done, 1)

        def mlp(c_, last=False):
            for j in range(4):
                n = 4 * c_ + j
                r = scr[:, (j % 2) * 512:(j % 2 + 1) * 512]
                s = scr[:, (2 + j % 2) * 512:(3 + j % 2) * 512]
                dve.wait_ge(act_relu, n + 1)
                V.tensor_tensor(s, r, r, ALU.mult).then_inc(act_sq, 1)
                dve.wait_ge(hid_hi, n + 1)
                dve.wait_ge(act_sq, n + 1)
                V.tensor_tensor(lat[:, 1, j, :], s, lat[:, 0, j, :].bitcast(F32),
                                ALU.subtract).then_inc(hid_lo, 1)
            if last:
                dve.wait_ge(row_full[3], 16)
            for m in range(16):
                t = m % TT
                dve.wait_ge(dn_ps, 16 * c_ + m + 1)
                V.tensor_tensor(block(m), block(m), ps[:, 4 + t, :], ALU.add).then_inc(dn_added, 1)
                if last and 2 <= m <= 12:
                    gated(m - 2)
                if last and m == 12:
                    gated(11)
                if last and m > 12:
                    out_tile(m % TT - 1, 1)
                if last and m >= 12:
                    out_tile(t, 0)
            if last:
                out_tile(TT - 1, 1)

        with dve.Fori(0, CHUNKS - 1) as c_:
            mlp(c_)
        mlp(CHUNKS - 1, True)


    @block.tensor
    def _(pe):
        pe.wait_ge(par_full, 16 * 8)
        pe.wait_ge(consts, 7)
        nc.tensor.transpose(ps[:, 7, 0:N_B], scr[0:N_B, 0:P], ident[0:N_B, 0:N_B])
        n2 = N_PC - N_B
        nc.tensor.transpose(ps[:, 7, N_B:N_PC], scr[0:n2, P:2 * P], ident[0:n2, 0:n2]).then_inc(par_ps, 1)

        pe.wait_ge(xn_done, TT)
        for k in range(KT):
            if k >= 4:
                pe.wait_ge(xt_out, k - 3)
            for t in range(TT):
                op = nc.tensor.transpose(ps[:, k % 4, t * P:(t + 1) * P], y[:, t, k * P:(k + 1) * P], ident[:])
            op.then_inc(xt_ps, 1)

        def col_sum(chunk, which, b, o):
            pe.wait_ge(ada_step, 16 * (chunk + 1))
            for i in range(4):
                op = nc.tensor.matmul(ps[:, b, o + i:o + i + 1], acc[:, which, i * P:(i + 1) * P], ones[:, 0:1],
                                      start=True, stop=True)
            op.then_inc(col_ps, 1)

        pe.wait_ge(ones_done, 1)
        pe.wait_ge(par_cols, 1)
        def down(kk, k0, k1, chunk=None):
            for u, tiles in ((U_A[kk], range(0, 4)), (U_B[kk], range(4, 7))):
                if chunk and tiles[0]:
                    pe.wait_ge(col_saved, chunk)
                    col_sum(chunk, chunk % 2, 7, 0)
                pe.wait_ge(lo_done, u + 1)
                w = halves(u % 2, 4, 512 if tiles[0] == 0 else 384)
                for k in range(k0, k1):
                    if tiles[0] == 0:
                        pe.wait_ge(h_lo, 4 * kk + k + 1)
                    last = kk == 3 and k == 3
                    for j, b in enumerate(tiles):
                        op = product(ps[:, b, :], [v[:, k, j * P:(j + 1) * P] for v in w], h_of(4 * kk + k),
                                     kk == 0 and k == 0, last)
                        if last:
                            op.then_inc(down_ps, 1)
                        elif kk < 3 and k == 3 and j == len(tiles) - 1:
                            op.then_inc(unit_used, 1)

        for kk in range(3):
            if kk:
                pe.wait_ge(col_saved, 2 * kk)
            col_sum(2 * kk, 0, 7, 0)
            col_sum(2 * kk + 1, 1, 7, 4)
            if kk == 0:
                pe.wait_ge(xt_out, KT)
            down(kk, 0, 4, 6 if kk == 2 else None)
        down(3, 0, 2, 7)
        down(3, 2, 4)

        def latent_sum(i):
            pe.wait_ge(sq_sum, i + 1)
            nc.tensor.matmul(ps[:, 7, :], ones[:], lat_square(4 * i), start=True, stop=True).then_inc(lat_sum, 1)

        pe.wait_ge(col_saved, 8)
        for i in (0, 1):
            pe.wait_ge(lo_done, U_C[i] + 1)
            w = halves(i, 8, 256)
            for part in (0, 1):
                b = (0, 3)[part]
                if i == 0:
                    pe.wait_ge(lat_out, b + 1)
                for k in range(8):
                    op = product(ps[:, b, :], [v[:, k, part * P:(part + 1) * P] for v in w], h_of(8 * i + k),
                                 i == 0 and k == 0, i == 1 and k == 7)
                if i == 1:
                    op.then_inc(down_ps if part == 0 else kr_ps, 1)
                elif part == 1:
                    op.then_inc(unit_used, 1)
            if i == 1:
                pe.wait_ge(lat_var, 1)
            latent_sum(i)

        def wo_tile(q, m, w, at=None):
            n, t = at or divmod(m, TT)
            banks = 4 if at else 2
            if m >= banks:
                pe.wait_ge(wo_added, 16 * q + m + 1 - banks)
            elif at:
                pe.wait_ge(pj_lo, 7 * PAIRS)
                pe.wait_ge(s_exp, 2 * PAIRS)
                pe.wait_ge(wo_added, 16 * q)
            else:
                pe.wait_ge(pj_lo, 7 * (q + 1) + 4 + m)
            for k in (0, 1):
                st = [big[:, S_AO[i] + k, t * P:(t + 1) * P] for i in (0, 1)]
                mv = [v[:, k, (n % 2) * 512:(n % 2 + 1) * 512] for v in w]
                op = product(ps[:, m % banks, :], st, mv, k == 0, k == 1)
            op.then_inc(wo_ps, 1)

        def pair(p):
            first = isinstance(p, int) and p == 0
            u = u_pair(p)
            wq = halves(0, 4, 2 * QD)
            wkv = halves(1, 4, 2 * KVD)

            def proj(k, b, w_cols, w, base):
                for kt in range(4):
                    op = product(ps[:, b, :], [w_cols(v[:, kt, :]) for v in w],
                                 (lat[:, 0, base + kt, :], lat[:, 1, base + kt, :]), kt == 0, kt == 3)
                op.then_inc(pj_ps, 1)
                return op

            pe.wait_ge(lo_done, u + 1)
            if first:
                pe.wait_ge(lat_lo, 4)
                pe.wait_ge(lat_out, 7)
            else:
                pe.wait_ge(s_exp, 2 * p)
            proj(0, 2, lambda v: v[:, 0:P], wq, 0)
            if first:
                pe.wait_ge(lat_out, 8)
            else:
                pe.wait_ge(wo_added, 16 * (p - 1))
                pe.wait_ge(pj_lo, 7 * p)
            proj(1, 0, lambda v: v[:, P:2 * P], wq, 0)
            if not first:
                col_sum(7 + 2 * p, 1, 5, 0)
            proj(2, 1, lambda v: v[:, 2 * P:3 * P], wq, 0)
            pe.wait_ge(lo_done, u + 2)
            pe.wait_ge(pj_lo, 7 * p + 2)
            if first:
                pe.wait_ge(kv_lo, 4)
            proj(3, 0, lambda v: v[:, 0:NOPE], wkv, 4)
            pe.wait_ge(pj_lo, 7 * p + 3)
            proj(4, 1, lambda v: v[:, KVD:KVD + NOPE], wkv, 4)

            def scores(hd):
                pe.wait_ge(pj_lo, 7 * p + 4 + hd)
                if first and hd == 0:
                    pe.wait_ge(kr_lo, 1)
                if hd == 1:
                    pe.wait_ge(s_exp, 2 * p + 1)
                elif not first:
                    pe.wait_ge(s_exp, 2 * p)
                    pe.wait_ge(ao_lo, 2 * p)
                for i in range(TT):
                    b, o = S_AT[i]
                    ln = (i + 1) * P
                    q = slice(i * P, (i + 1) * P)
                    st = [big[:, s + hd, q] for s in S_QN]
                    mv = [big[:, s + hd, 0:ln] for s in S_KN]
                    product(ps[:, b, o:o + ln], st, mv, True, False)
                    nc.tensor.matmul(ps[:, b, o + i * P:o + ln], mask_u[:], mask_v[:], start=False, stop=False)
                    op = product(ps[:, b, o:o + ln], [big[:, s, q] for s in S_QR],
                                 [krope[:, hd, s, 0:ln] for s in (0, 1)], False, True)
                op.then_inc(s_ps, 1)

            def values():
                for t in range(TT):
                    b, o = 5 + t // 2, (t % 2) * 256
                    if t == 0 and first:
                        pe.wait_ge(lat_out, 7)
                    elif t == 0:
                        pe.wait_ge(col_saved, 8 + 2 * p)
                        pe.wait_ge(t_lo, 2 * p)
                    for kt in range(4):
                        st = [lat[:, i, 4 + kt, t * P:(t + 1) * P] for i in (0, 1)]
                        mv = [v[:, kt, :].rearrange("p (d n) -> p d n", d=2)[:, :, NOPE:] for v in wkv]
                        op = product(ps[:, b, o:o + 256], st, mv, kt == 0, kt == 3)
                    if t % 2 == 1:
                        op.then_inc(pj_ps, 1)

            def turn(hd):
                pe.wait_ge(p_norm, 2 * p + hd + 1)
                if hd == 1:
                    pe.wait_ge(t_lo, 2 * p + 1)
                    pe.wait_ge(col_saved, 8 + 2 * p + 1)
                else:
                    pe.wait_ge(pj_lo, 7 * p + 7)
                    if not first:
                        pe.wait_ge(ao_lo, 2 * p)
                for i in T_ORDER:
                    b, o = t_at(i, hd)
                    for j in range(i + 1):
                        src = scr[:, P_AT[i] + j * P:P_AT[i] + (j + 1) * P]
                        op = nc.tensor.transpose(ps[:, b, o + j * P:o + (j + 1) * P], src, ident[:])
                op.then_inc(t_ps, 1)

            def weighted(hd):
                pe.wait_ge(t_lo, 2 * p + hd + 1)
                pe.wait_ge(pj_lo, 7 * p + 7)
                b = (7, 4)[hd]
                for j in range(TT):
                    st = [v_view(i)[:, j, hd * VDIM:(hd + 1) * VDIM] for i in (0, 1)]
                    mv = [big[:, S_PT[i] + j, j * P:TOK] for i in (0, 1)]
                    op = product(ps[:, b, j * P:TOK], st, mv, j == 0, j == TT - 1)
                op.then_inc(pv_ps, 1)

            def wo_block(n, w):
                for t in range(TT):
                    wo_tile(p - 1, 4 * n + t, w)

            wo = [halves(s, 2, 1024) for s in (0, 1)]
            scores(0)
            values()
            if not first:
                pe.wait_ge(lo_done, u + 3)
                pe.wait_ge(ao_lo, 2 * p)
                wo_block(0, wo[0])
            turn(0)
            scores(1)
            if not first:
                wo_block(1, wo[0])
            weighted(0)
            col_sum(8 + 2 * p, 0, 5, 0)
            if not first:
                pe.wait_ge(lo_done, u + 4)
                wo_block(2, wo[1])
            turn(1)
            if not first:
                wo_block(3, wo[1])
            weighted(1)

        pair(0)
        with pe.Fori(1, PAIRS) as p:
            pair(p)
        pe.wait_ge(lo_done, U_MLP - 1)
        pe.wait_ge(ao_lo, 2 * PAIRS)
        w_two = [halves(s, 2, 1024) for s in (0, 1)]
        for order, (t, n) in enumerate(LAST_WO):
            if order == 4:
                pe.wait_ge(lo_done, U_MLP)
            wo_tile(PAIRS - 1, order, w_two[n // 2], (n, t))
            if order == 1:
                col_sum(7 + 2 * PAIRS, 1, 5, 0)
            if order == 3:
                pe.wait_ge(four_done, 1)
                nc.tensor.transpose(ps[0:4 * KT, 5, 0:P], four[:].rearrange("p s k -> p (s k)"),
                                    ident[:]).then_inc(four_ps, 1)

        def turn_h(t):
            pe.wait_ge(h_mul, t + 1)
            if t == 0:
                pe.wait_ge(ao_lo, 2 * PAIRS)
                pe.wait_ge(four_out, 1)
            elif t == 1:
                pe.wait_ge(wo_added, 16 * PAIRS)
            else:
                pe.wait_ge(h_lo, KT + 4 * (1 if t == 2 else 3))
            for g in range(4):
                for k in range(4 * g, 4 * g + 4):
                    op = nc.tensor.transpose(ps[:, turn_bank(t) + g, (k % 4) * P:(k % 4 + 1) * P],
                                             y[:, t, k * P:(k + 1) * P], ident[:])
                op.then_inc(xt_ps, 1)

        def up_part(u, kk, a, b):
            pe.wait_ge(lo_done, u + kk + 1)
            w = halves(kk % 2, 4, 512)
            for j in range(4):
                for k in range(4):
                    op = product(ps[:, j, a:b], [v[:, k, j * P:(j + 1) * P] for v in w],
                                 [v[:, a:b] for v in h_of(4 * kk + k)], kk == 0 and k == 0 and a == 0,
                                 kk == 3 and k == 3)
                if kk == 3:
                    op.then_inc(up_ps, 1)
            if kk < 3 and b == TOK:
                op.then_inc(unit_used, 1)

        def mlp(c_):
            first = isinstance(c_, int)
            u = U_MLP + 8 * c_
            for kk in range(4):
                if kk == 0 and not first:
                    pe.wait_ge(act_sq, 4 * c_)
                    pe.wait_ge(hid_hi, 4 * c_)
                if first and kk < 2:
                    up_part(u, kk, TOK // 2, TOK)
                else:
                    up_part(u, kk, 0, TOK)
            for n in range(4):
                pe.wait_ge(lo_done, u + 5 + n)
                w = halves(n % 2, 4, 512)
                order = ([(k, t) for k in range(4) for t in range(TT)] if n == 0 else
                         [(k, t) for t in range(TT) for k in range(4)])
                for k, t in order:
                    if n == 0 and t == 0:
                        pe.wait_ge(hid_lo, 4 * c_ + k + 1)
                    if k == 0 and not (first and n == 0):
                        pe.wait_ge(dn_added, 16 * c_ + 4 * n - 4 + t + 1)
                    st = [lat[:, i, k, t * P:(t + 1) * P] for i in (0, 1)]
                    op = product(ps[:, 4 + t, :], st, [v[:, k, :] for v in w], k == 0, k == 3)
                    if k == 3:
                        op.then_inc(dn_ps, 1)

        turn_h(0)
        turn_h(1)
        turn_h(2)
        pe.wait_ge(h_lo, KT + 4 * 2)
        up_part(U_MLP, 0, 0, TOK // 2)
        turn_h(3)
        up_part(U_MLP, 1, 0, TOK // 2)
        pe.wait_ge(h_lo, KT + 4 * TT)
        mlp(0)
        with pe.Fori(1, CHUNKS) as c_:
            mlp(c_)

    ctx.close()


_INS = ["x", "c", "positions", "ada_w", "ada_b", "norm_pre", "norm_post", "mla_w_down", "mla_q_norm",
        "mla_w_uq", "mla_kv_norm", "mla_w_ukv", "mla_w_o", "mlp_up", "mlp_down"]


def kernel(**inputs):
    import numpy as _np
    import concourse.bacc as _bacc
    from concourse import mybir as _mybir
    from concourse.bass_utils import run_bass_kernel_spmd as _run

    nc = _bacc.Bacc("TRN2", target_bir_lowering=False, num_devices=1, dynamic_dma_scratch_size=1024)
    arrays, args = {}, []
    freq = _np.float32(10000.0) ** (-_np.arange(0, 64, 2, dtype=_np.float32) / _np.float32(64))
    consts = {"inv_freq": _np.tile(freq.astype(_np.float32), 4).reshape(128, 1)}
    for name in _INS + ["inv_freq"]:
        a = _np.ascontiguousarray(consts[name] if name in consts else inputs[name])
        arrays[f"in_{name}_dram"] = a
        args.append(nc.dram_tensor(f"in_{name}_dram", a.shape, _mybir.dt.from_np(a.dtype), kind="ExternalInput").ap())
    out = nc.dram_tensor("out_0_dram", (1, 512, 2048), _mybir.dt.float32, kind="ExternalOutput").ap()
    trunk(nc, *args, out)
    r = _run(nc, [arrays], core_ids=[0])
    return r.results[0]["out_0_dram"]
```
